# Optimizing a Trainium2 kernel written in Bass

```python
import math
import jax, jax.numpy as jnp
from jax import lax
import numpy as np

D_MODEL = 1024
BATCH = 1
SEQ = 512
DEPTH = 1
DEC_BATCH = 1
DEC_SEQ = 2048
PAST_LEN = 128

N_MEM = 256
BRANCH_W = 512
N_BRANCH = 3
EPS = 1e-6
GLA_HEADS = 4
GLA_DK = 64
GLA_DV = 128
GLA_RANK = 16
GLA_TAU = 16.0
GLA_CHUNK = 64
GLA_Q = GLA_HEADS * GLA_DK
GLA_V = GLA_HEADS * GLA_DV
DIFF_HEADS = 4
DIFF_HD = 64
DIFF_DV = 2 * DIFF_HD
DIFF_QK = DIFF_HEADS * 2 * DIFF_HD
DIFF_V = DIFF_HEADS * DIFF_DV
Q_BLOCK = 128
CROSS_HEADS = 4
CROSS_HD = 128
CROSS_Q = CROSS_HEADS * CROSS_HD
SPLITS = (GLA_Q, GLA_Q, GLA_V, 2 * GLA_RANK, BRANCH_W,
          DIFF_QK, DIFF_QK, DIFF_V, BRANCH_W,
          CROSS_Q, BRANCH_W, N_BRANCH * D_MODEL)
IN_COLS = GLA_Q * 2 + GLA_V + 2 * GLA_RANK + BRANCH_W + DIFF_QK * 2 + DIFF_V + BRANCH_W + CROSS_Q + BRANCH_W + N_BRANCH * D_MODEL

kernel_name = "hybrid_gla_diffattn_memxattn_encoder"

def rmsnorm(x, g):
    xf = x.astype(jnp.float32)
    y = xf * lax.rsqrt(jnp.mean(xf * xf, axis=-1, keepdims=True) + EPS)
    return (y * g.astype(jnp.float32)).astype(x.dtype)

def gla_scan(q, k, v, log_a):
    B, H, T, DK = q.shape
    DV = v.shape[-1]
    n = T // GLA_CHUNK

    def to_chunks(a):
        return jnp.moveaxis(a.reshape(B, H, n, GLA_CHUNK, a.shape[-1]), 2, 0)

    mask = jnp.tril(jnp.ones((GLA_CHUNK, GLA_CHUNK), dtype=bool))[:, :, None]

    def step(S, inp):
        qc, kc, vc, ac = inp
        b = jnp.cumsum(ac, axis=2)
        o_inter = jnp.einsum('bhtd,bhdv->bhtv', qc * jnp.exp(b), S)
        diff = b[:, :, :, None, :] - b[:, :, None, :, :]
        decay = jnp.exp(jnp.where(mask, diff, -jnp.inf))
        att = jnp.einsum('bhtd,bhsd,bhtsd->bhts', qc, kc, decay)
        o = o_inter + jnp.einsum('bhts,bhsv->bhtv', att, vc)
        b_last = b[:, :, -1:, :]
        S = jnp.exp(b_last[:, :, 0, :])[..., None] * S + jnp.einsum(
            'bhsd,bhsv->bhdv', kc * jnp.exp(b_last - b), vc)
        return S, o

    S0 = jnp.zeros((B, H, DK, DV), jnp.float32)
    _, o = lax.scan(step, S0, (to_chunks(q), to_chunks(k), to_chunks(v), to_chunks(log_a)))
    return jnp.moveaxis(o, 0, 2).reshape(B, H, T, DV)

def gla_branch(q, k, v, glr, w2, b2, g_norm):
    B, T, _ = q.shape

    def heads(a, d):
        return a.reshape(B, T, GLA_HEADS, d).transpose(0, 2, 1, 3).astype(jnp.float32)

    qh = heads(q, GLA_DK) * (GLA_DK ** -0.5)
    kh = heads(k, GLA_DK)
    vh = heads(v, GLA_DV)
    glr = glr.astype(jnp.float32).reshape(B, T, 2, GLA_RANK)
    gate_logits = jnp.einsum('btir,irk->btik', glr, w2.astype(jnp.float32)) + b2.astype(jnp.float32)
    log_a = jax.nn.log_sigmoid(gate_logits) / GLA_TAU
    la_f = heads(log_a[:, :, 0], GLA_DK)
    la_b = heads(log_a[:, :, 1], GLA_DK)
    flip = lambda a: jnp.flip(a, axis=2)
    o_f = gla_scan(qh, kh, vh, la_f)
    o_b = flip(gla_scan(flip(qh), flip(kh), flip(vh), flip(la_b)))
    o = rmsnorm(o_f + o_b, g_norm)
    return o.transpose(0, 2, 1, 3).reshape(B, T, GLA_V)

def diff_attention(q, k, v, lam_params, g_norm, lambda_init):
    B, T, _ = q.shape
    H, HD = DIFF_HEADS, DIFF_HD
    qh = q.reshape(B, T, H, 2, HD).transpose(3, 0, 2, 1, 4).astype(jnp.float32) * (HD ** -0.5)
    kh = k.reshape(B, T, H, 2, HD).transpose(3, 0, 2, 1, 4).astype(jnp.float32)
    vh = v.reshape(B, T, H, DIFF_DV).transpose(0, 2, 1, 3).astype(jnp.float32)
    lp = lam_params.astype(jnp.float32)
    lam = jnp.exp(jnp.sum(lp[0] * lp[1])) - jnp.exp(jnp.sum(lp[2] * lp[3])) + lambda_init
    slopes = 2.0 ** (-8.0 * (jnp.arange(H, dtype=jnp.float32) + 1.0) / H)
    pos = jnp.arange(T, dtype=jnp.float32)
    nb = T // Q_BLOCK
    qb = qh.reshape(2, B, H, nb, Q_BLOCK, HD).transpose(3, 0, 1, 2, 4, 5)
    starts = jnp.arange(nb, dtype=jnp.int32) * Q_BLOCK

    def block(inp):
        qblk, t0 = inp
        tq = t0.astype(jnp.float32) + jnp.arange(Q_BLOCK, dtype=jnp.float32)
        bias = -slopes[:, None, None] * jnp.abs(tq[:, None] - pos[None, :])
        s = jnp.einsum('ibhqd,ibhkd->ibhqk', qblk, kh) + bias
        p = jax.nn.softmax(s, axis=-1)
        a = p[0] - lam * p[1]
        return jnp.einsum('bhqk,bhkv->bhqv', a, vh)

    o = lax.map(block, (qb, starts))
    o = o.transpose(1, 2, 0, 3, 4).reshape(B, H, T, DIFF_DV)
    o = rmsnorm(o, g_norm) * (1.0 - lambda_init)
    return o.transpose(0, 2, 1, 3).reshape(B, T, DIFF_V)

def memory_cross_attention(q, mem, mem_norm_g, w_kv):
    B, T, _ = q.shape
    M = mem.shape[1]
    m = rmsnorm(mem, mem_norm_g)
    kv = jnp.einsum('bmd,de->bme', m, w_kv)
    kh = kv[..., :CROSS_Q].reshape(B, M, CROSS_HEADS, CROSS_HD).astype(jnp.float32)
    vh = kv[..., CROSS_Q:].reshape(B, M, CROSS_HEADS, CROSS_HD).astype(jnp.float32)
    qh = q.reshape(B, T, CROSS_HEADS, CROSS_HD).astype(jnp.float32) * (CROSS_HD ** -0.5)
    p = jax.nn.softmax(jnp.einsum('bthd,bmhd->bhtm', qh, kh), axis=-1)
    o = jnp.einsum('bhtm,bmhd->bthd', p, vh)
    return o.reshape(B, T, CROSS_Q)

def trunk(x, mem, norm_g, w_in, gla_gate_w2, gla_gate_b, gla_norm_g, diff_lambda,
          diff_norm_g, mem_norm_g, w_mem_kv, w_branch, w_out, final_norm_g):
    B, T, D = x.shape
    offsets = [int(o) for o in np.cumsum(np.array(SPLITS))[:-1]]
    for l in range(DEPTH):
        lambda_init = 0.8 - 0.6 * math.exp(-0.3 * l)
        h = rmsnorm(x, norm_g[l])
        proj = jnp.einsum('btd,de->bte', h, w_in[l])
        (g_q, g_k, g_v, g_lr, z_a, d_q, d_k, d_v, z_b, c_q, z_c, gate_in) = jnp.split(proj, offsets, axis=-1)
        o_a = gla_branch(g_q, g_k, g_v, g_lr, gla_gate_w2[l], gla_gate_b[l], gla_norm_g[l]).astype(x.dtype) * jax.nn.silu(z_a)
        o_b = diff_attention(d_q, d_k, d_v, diff_lambda[l], diff_norm_g[l], lambda_init).astype(x.dtype) * jax.nn.silu(z_b)
        o_c = memory_cross_attention(c_q, mem, mem_norm_g[l], w_mem_kv[l]).astype(x.dtype) * jax.nn.silu(z_c)
        branches = jnp.stack([o_a, o_b, o_c], axis=2)
        gates = jax.nn.sigmoid(gate_in.reshape(B, T, N_BRANCH, D))
        merged = jnp.sum(gates * jnp.einsum('btiw,iwd->btid', branches, w_branch[l]), axis=2)
        x = x + jnp.einsum('btd,de->bte', merged, w_out[l])
    return rmsnorm(x, final_norm_g)

def setup_inputs(seed: int = 0) -> dict:
    key = jax.random.key(seed)
    ks = jax.random.split(key, 17)
    f32 = jnp.float32
    nrm = lambda k, s: jax.random.normal(k, s, f32)
    return {
        "x_prompt": nrm(ks[0], (BATCH, SEQ, D_MODEL)),
        "x_sample": nrm(ks[1], (DEC_BATCH, DEC_SEQ, D_MODEL)),
        "mem_prompt": nrm(ks[2], (BATCH, N_MEM, D_MODEL)),
        "mem_sample": nrm(ks[3], (DEC_BATCH, N_MEM, D_MODEL)),
        "norm_g": 1.0 + 0.02 * nrm(ks[4], (DEPTH, D_MODEL)),
        "w_in": nrm(ks[5], (DEPTH, D_MODEL, IN_COLS)) * D_MODEL ** -0.5,
        "gla_gate_w2": nrm(ks[6], (DEPTH, 2, GLA_RANK, GLA_Q)) * GLA_RANK ** -0.5,
        "gla_gate_b": 0.1 * nrm(ks[7], (DEPTH, 2, GLA_Q)),
        "gla_norm_g": 1.0 + 0.02 * nrm(ks[8], (DEPTH, GLA_DV)),
        "diff_lambda": 0.1 * nrm(ks[9], (DEPTH, 4, DIFF_HD)),
        "diff_norm_g": 1.0 + 0.02 * nrm(ks[10], (DEPTH, DIFF_DV)),
        "mem_norm_g": 1.0 + 0.02 * nrm(ks[11], (DEPTH, D_MODEL)),
        "w_mem_kv": nrm(ks[12], (DEPTH, D_MODEL, 2 * CROSS_Q)) * D_MODEL ** -0.5,
        "w_branch": nrm(ks[13], (DEPTH, N_BRANCH, BRANCH_W, D_MODEL)) * BRANCH_W ** -0.5,
        "w_out": nrm(ks[14], (DEPTH, D_MODEL, D_MODEL)) * D_MODEL ** -0.5,
        "final_norm_g": 1.0 + 0.02 * nrm(ks[15], (D_MODEL,)),
    }

def reference(x_prompt, x_sample, mem_prompt, mem_sample, norm_g, w_in, gla_gate_w2, gla_gate_b,
              gla_norm_g, diff_lambda, diff_norm_g, mem_norm_g, w_mem_kv, w_branch, w_out, final_norm_g):
    y_prompt = trunk(x_prompt, mem_prompt, norm_g, w_in, gla_gate_w2, gla_gate_b, gla_norm_g, diff_lambda,
                     diff_norm_g, mem_norm_g, w_mem_kv, w_branch, w_out, final_norm_g)
    y_sample = trunk(x_sample, mem_sample, norm_g, w_in, gla_gate_w2, gla_gate_b, gla_norm_g, diff_lambda,
                     diff_norm_g, mem_norm_g, w_mem_kv, w_branch, w_out, final_norm_g)
    return (y_prompt, y_sample)


_drawn_inputs = setup_inputs


def setup_inputs(seed=0):
    import zlib

    import numpy as np

    out = dict(_drawn_inputs(seed))
    spreads = {}
    factors = {'norm_g': 3.57,
     'gla_gate_b': 4.502,
     'gla_norm_g': 8.0,
     'diff_lambda': 8.0,
     'diff_norm_g': 8.0,
     'mem_norm_g': 8.0,
     'final_norm_g': 2.859}
    for name, (base, spread) in spreads.items():
        noise = np.random.default_rng([zlib.crc32(name.encode()), seed]).standard_normal(out[name].shape)
        drawn = base * np.exp(spread * noise) if base else spread * noise
        out[name] = __import__('jax').numpy.asarray(drawn.astype(out[name].dtype))
    for name, factor in factors.items():
        out[name] = (out[name] * factor).astype(out[name].dtype)
    return out
```

```python
import concourse.bass as bass
from concourse import mybir
from contextlib import ExitStack
import numpy as np

FP32 = mybir.dt.float32
FP32R = mybir.dt.float32r
I32 = mybir.dt.int32
ALU = mybir.AluOpType
ACT = mybir.ActivationFunctionType
AXX = mybir.AxisListType.X

P = 128
D = 1024
KT = D // P
SEQS = (512, 2048)
TOK = sum(SEQS)
N_MEM = 256
MEM = 2 * N_MEM
ROWS = TOK + MEM
CH = 512
EPS = 1e-6
LAMBDA_INIT = 0.2

H = 4
GK = 64
GV = 128
RANK = 16
TAU = 16.0
W = 512
N_FEAT = 16
GQ_BLOCK, GK_BLOCK, DQ_BLOCK, DK_BLOCK, CQ_BLOCK = 0, 2, 4, 8, 12
SLOPES = [2.0 ** (-8.0 * (h + 1) / H) for h in range(H)]
ALIBI_MID = max(SEQS) - P
ALIBI_W = ALIBI_MID + max(SEQS)
LEVELS = (64, 32, 16, 8, 4, 2, 1)


class Mem:

    def __init__(self, nc, ctx, phase):
        self.nc, self.ctx, self.phase = nc, ctx, phase
        self.allocated = []

    def sb(self, name, shape, dtype=FP32):
        return self.ctx.enter_context(self.nc.sbuf_tensor(f"{self.phase}_{name}", shape, dtype))

    def ps(self, name, shape):
        return self.ctx.enter_context(self.nc.psum_tensor(f"{self.phase}_{name}", shape, FP32))

    def sem(self, name):
        s = self.nc.alloc_semaphore(f"{self.phase}_{name}")
        self.allocated.append(s)
        return s

    def block(self):
        def clear():
            self.nc.clear_and_free_semaphores(self.allocated)
            self.nc.all_engine_barrier()

        self.ctx.callback(clear)
        return self.ctx.enter_context(self.nc.Block())

    def sems(self, name, n):
        return [self.sem(f"{name}{i}") for i in range(n)]


def rows(ap, start, n):
    return ap[bass.ds(start, n), :]


def block3(ap, i):
    return ap[bass.ds(i, 1)].rearrange("o p k c -> p (o k) c")


class Chain:

    def __init__(self, engine, semaphore, base=0):
        self.engine, self.semaphore, self.base, self.n = engine, semaphore, base, 0

    def __call__(self, instruction):
        self.n += 1
        instruction.then_inc(self.semaphore, 1)
        self.engine.wait_ge(self.semaphore, self.base + self.n)


RSQRT_STEPS = 11


def rsqrt(step, dve, out, v, tmp):
    step(dve.tensor_scalar(tmp.bitcast(I32), v.bitcast(I32), 1, None, ALU.logical_shift_right))
    step(dve.tensor_scalar(out.bitcast(I32), tmp.bitcast(I32), -1.0, float(0x5F3759DF), ALU.mult, ALU.add))
    for _ in range(3):
        step(dve.tensor_tensor(tmp, out, out, ALU.mult))
        step(dve.scalar_tensor_tensor(tmp, tmp, -0.5, v, ALU.mult, ALU.mult))
        step(dve.scalar_tensor_tensor(out, tmp, 1.5, out, ALU.add, ALU.mult))


def product3(pe, out, a_hi, a_lo, b_hi, b_lo, first, last):
    pe.matmul(out, a_hi, b_hi, start=first, stop=False)
    pe.matmul(out, a_hi, b_lo, start=False, stop=False)
    return pe.matmul(out, a_lo, b_hi, start=False, stop=last)


def phase_norm(nc, x_all, gains, ident_dram, hT_hi, hT_lo):
    with ExitStack() as ctx:
        m = Mem(nc, ctx, "norm")
        B = 2
        x = m.sb("x", [P, B, D])
        xn = m.sb("xn", [P, B, D])
        sq = m.sb("sq", [P, D])
        gain = m.sb("gain", [P, 2, D])
        ident = m.sb("ident", [P, P])
        stat = m.sb("stat", [P, B, 4])
        hi = m.sb("hi", [P, B, KT, P], FP32R)
        lo = m.sb("lo", [P, B, KT, P], FP32R)
        tp = m.ps("tp", [P, B, 2, 512])
        consts_in = m.sem("consts_in")
        x_in = m.sems("x_in", B)
        squares = m.sem("squares")
        normed = m.sem("normed")
        transposed = m.sem("transposed")
        hi_ready = m.sem("hi_ready")
        lo_ready = m.sem("lo_ready")
        hi_out = m.sems("hi_out", B)
        lo_out = m.sems("lo_out", B)
        steps = m.sem("steps")
        block = m.block()
        n_x, n_mem = TOK // P // B, MEM // P // B
        n = n_x + n_mem
        PER = RSQRT_STEPS + 1

        @block.sync
        def _(sp):
            sp.dma_start(gain[:, :, :], gains).then_inc(consts_in, 16)
            sp.dma_start(ident[:, :], ident_dram).then_inc(consts_in, 16)
            with sp.Fori(0, n) as i:
                for b in range(B):
                    sp.wait_ge(normed, i * B)
                    sp.dma_start(x[:, b, :], rows(x_all, i * (B * P) + b * P, P)).then_inc(x_in[b], 16)

        @block.scalar
        def _(act):
            with act.Fori(0, n) as i:
                for b in range(B):
                    act.wait_ge(x_in[b], i * 16 + 16)
                    act.wait_ge(normed, i * B)
                    act.activation(sq[:, :], x[:, b, :], ACT.Square, accum_out=stat[:, b, 0:1]).then_inc(squares, 1)
                    act.wait_ge(transposed, i * B + (b + 1))
                    act.wait_ge(hi_out[b], i * 16)
                    for j in range(2):
                        done = act.activation(hi[:, b, 4 * j:4 * j + 4, :].rearrange("p k c -> p (k c)"), tp[:, b, j, :], ACT.Copy)
                    done.then_inc(hi_ready, 1)
                    act.wait_ge(hi_ready, i * B + (b + 1))
                    act.dma_start(hT_hi[:, :, bass.ds(i * (B * P) + b * P, P)].rearrange("k p t -> p k t"), hi[:, b].bitcast(FP32)).then_inc(hi_out[b], 16)
                    act.wait_ge(lo_ready, i * B + (b + 1))
                    act.dma_start(hT_lo[:, :, bass.ds(i * (B * P) + b * P, P)].rearrange("k p t -> p k t"), lo[:, b].bitcast(FP32)).then_inc(lo_out[b], 16)
            for b in range(B):
                act.wait_ge(hi_out[b], n * 16)
                act.wait_ge(lo_out[b], n * 16)

        @block.vector
        def _(dve):
            dve.wait_ge(consts_in, 32)
            for g, (i0, i1) in enumerate(((0, n_x), (n_x, n))):
                with dve.Fori(i0, i1) as i:
                    for b in range(B):
                        step = Chain(dve, steps, i * (B * PER) + b * PER)
                        dve.wait_ge(squares, i * B + (b + 1))
                        step(dve.tensor_scalar(stat[:, b, 1:2], stat[:, b, 0:1], 1.0 / D, EPS, ALU.mult, ALU.add))
                        rsqrt(step, dve, stat[:, b, 2:3], stat[:, b, 1:2], stat[:, b, 3:4])
                        dve.wait_ge(transposed, i * B)
                        dve.scalar_tensor_tensor(xn[:, b, :], x[:, b, :], stat[:, b, 2:3], gain[:, g, :],
                                                 ALU.mult, ALU.mult).then_inc(normed, 1)
                        dve.wait_ge(hi_ready, i * B + (b + 1))
                        dve.wait_ge(lo_out[b], i * 16)
                        for j in range(2):
                            half = slice(4 * j, 4 * j + 4)
                            done = dve.tensor_tensor(lo[:, b, half, :].rearrange("p k c -> p (k c)"), tp[:, b, j, :],
                                                     hi[:, b, half, :].rearrange("p k c -> p (k c)"), ALU.subtract)
                        done.then_inc(lo_ready, 1)

        @block.tensor
        def _(pe):
            pe.wait_ge(consts_in, 32)
            with pe.Fori(0, n) as i:
                for b in range(B):
                    pe.wait_ge(normed, i * B + (b + 1))
                    pe.wait_ge(lo_ready, i * B)
                    for k in range(KT):
                        done = pe.transpose(tp[:, b, k // 4, (k % 4) * P:(k % 4 + 1) * P], xn[:, b, k * P:(k + 1) * P], ident[:, :])
                    done.then_inc(transposed, 1)


def phase_project(nc, name, hT_hi, hT_lo, first_token, n_chunks, w_stream, n_stream, w_narrow, w_values, featT, narrowT, values):
    with ExitStack() as ctx:
        m = Mem(nc, ctx, name)
        NV, NN = len(w_values), len(w_narrow)
        SLOTS, BANKS, TT, COLS = 2, 4, CH // P, W // P
        n_resident = NN + NV * TT
        per = n_resident + n_stream
        n_split = NN + NV * COLS
        h_hi, h_lo = (m.sb(f"h_{s}", [P, KT, CH], FP32R) for s in ("hi", "lo"))
        raw = m.sb("raw", [P, SLOTS, KT, P])
        w_hi, w_lo = (m.sb(f"w_{s}", [P, SLOTS, KT, P], FP32R) for s in ("hi", "lo"))
        wn_hi, wn_lo = (m.sb(f"wn_{s}", [P, max(NN, 1), KT, P], FP32R) for s in ("hi", "lo"))
        wv_hi, wv_lo = (m.sb(f"wv_{s}", [P, NV, KT, W], FP32R) for s in ("hi", "lo"))
        out = m.sb("out", [P, SLOTS, CH])
        acc = m.ps("acc", [P, BANKS, CH])
        raw_in = m.sems("raw_in", SLOTS)
        h_in = m.sems("h_in", KT)
        hi_split = m.sem("hi_split")
        lo_split = m.sem("lo_split")
        unit_done = m.sem("unit_done")
        evacuated = m.sem("evacuated")
        stored = m.sems("stored", SLOTS)
        block = m.block()

        def resident_piece(u):
            if u < NN:
                return w_narrow[u], wn_hi[:, u], wn_lo[:, u]
            v, c = divmod(u - NN, COLS)
            cols = slice(c * P, (c + 1) * P)
            return w_values[v][:, :, cols], wv_hi[:, v, :, cols], wv_lo[:, v, :, cols]

        raw_slot = [(n_split + s) % SLOTS for s in range(SLOTS)]
        raw_before = [n_split // SLOTS + (r < n_split % SLOTS) for r in range(SLOTS)]
        out_slot = [(n_resident + s) % SLOTS for s in range(SLOTS)]
        out_before = [n_resident // SLOTS + (r < n_resident % SLOTS) for r in range(SLOTS)]
        out_per = [out_before[r] + n_stream // SLOTS for r in range(SLOTS)]

        @block.sync
        def _(sp):
            for u in range(n_split):
                if u >= SLOTS:
                    sp.wait_ge(lo_split, u + 1 - SLOTS)
                sp.dma_start(raw[:, u % SLOTS], resident_piece(u)[0]).then_inc(raw_in[u % SLOTS], 16)
            with sp.Fori(0, n_chunks) as c:
                sp.wait_ge(unit_done, c * per)
                for k in range(KT):
                    cols = bass.ds(c * CH + first_token, CH)
                    sp.dma_start(h_hi[:, k].bitcast(FP32), hT_hi[k][:, cols]).then_inc(h_in[k], 16)
                    sp.dma_start(h_lo[:, k].bitcast(FP32), hT_lo[k][:, cols]).then_inc(h_in[k], 16)
                with sp.Fori(0, n_stream // SLOTS) as i:
                    for s in range(SLOTS):
                        sp.wait_ge(lo_split, c * n_stream + i * SLOTS + (n_split + s + 1 - SLOTS))
                        sp.dma_start(raw[:, raw_slot[s]], block3(w_stream, i * SLOTS + s)).then_inc(raw_in[raw_slot[s]], 16)

        @block.vector
        def _(dve):
            for u in range(n_split):
                dve.wait_ge(raw_in[u % SLOTS], 16 * (u // SLOTS + 1))
                dve.tensor_copy(resident_piece(u)[1], raw[:, u % SLOTS]).then_inc(hi_split, 1)
            with dve.Fori(0, n_chunks) as c:
                with dve.Fori(0, n_stream // SLOTS) as i:
                    for s in range(SLOTS):
                        r = raw_slot[s]
                        dve.wait_ge(raw_in[r], c * (16 * (n_stream // SLOTS)) + i * 16 + 16 * (raw_before[r] + 1))
                        dve.wait_ge(unit_done, c * per + i * SLOTS + (n_resident + s + 1 - SLOTS))
                        dve.tensor_copy(w_hi[:, s], raw[:, r]).then_inc(hi_split, 1)

        @block.gpsimd
        def _(pool):
            for u in range(n_split):
                _, hi, lo = resident_piece(u)
                pool.wait_ge(hi_split, u + 1)
                pool.tensor_tensor(lo, raw[:, u % SLOTS], hi, ALU.subtract).then_inc(lo_split, 1)
            with pool.Fori(0, n_chunks) as c:
                with pool.Fori(0, n_stream // SLOTS) as i:
                    for s in range(SLOTS):
                        pool.wait_ge(hi_split, c * n_stream + i * SLOTS + (n_split + s + 1))
                        pool.tensor_tensor(w_lo[:, s], raw[:, raw_slot[s]], w_hi[:, s], ALU.subtract).then_inc(lo_split, 1)

        @block.tensor
        def _(pe):
            with pe.Fori(0, n_chunks) as c:
                for u in range(n_resident):
                    pe.wait_ge(evacuated, c * per + max(u + 1 - BANKS, 0))
                    if u < NN:
                        pe.wait_ge(lo_split, u + 1)
                    elif (u - NN) % TT == 0:
                        pe.wait_ge(lo_split, NN + ((u - NN) // TT + 1) * COLS)
                    for k in range(KT):
                        if u == 0:
                            pe.wait_ge(h_in[k], c * 32 + 32)
                        if u < NN:
                            operands = (wn_hi[:, u, k], wn_lo[:, u, k], h_hi[:, k], h_lo[:, k])
                        else:
                            v, t = divmod(u - NN, TT)
                            tok = slice(t * P, (t + 1) * P)
                            operands = (h_hi[:, k, tok], h_lo[:, k, tok], wv_hi[:, v, k], wv_lo[:, v, k])
                        done = product3(pe, acc[:, u % BANKS], *operands, k == 0, k == KT - 1)
                    done.then_inc(unit_done, 1)
                with pe.Fori(0, n_stream // BANKS) as i:
                    for b in range(BANKS):
                        s = b % SLOTS
                        pe.wait_ge(evacuated, c * per + i * BANKS + (n_resident + b + 1 - BANKS))
                        pe.wait_ge(lo_split, c * n_stream + i * BANKS + (n_split + b + 1))
                        for k in range(KT):
                            done = product3(pe, acc[:, (n_resident + b) % BANKS], w_hi[:, s, k], w_lo[:, s, k],
                                            h_hi[:, k], h_lo[:, k], k == 0, k == KT - 1)
                        done.then_inc(unit_done, 1)

        @block.scalar
        def _(act):
            act.preload_act_table(ACT.Exp)
            with act.Fori(0, n_chunks) as c:
                for u in range(n_resident):
                    s = u % SLOTS
                    act.wait_ge(unit_done, c * per + (u + 1))
                    act.wait_ge(stored[s], c * (16 * out_per[s]) + 16 * (u // SLOTS))
                    act.activation(out[:, s], acc[:, u % BANKS], ACT.Copy).then_inc(evacuated, 1)
                    act.wait_ge(evacuated, c * per + (u + 1))
                    if u < NN:
                        dst = narrowT[u][:, bass.ds(c * CH, CH)]
                    else:
                        v, t = divmod(u - NN, TT)
                        dst = values[v][bass.ds(c * CH + t * P, P), :]
                    act.dma_start(dst, out[:, s]).then_inc(stored[s], 16)
                with act.Fori(0, n_stream // BANKS) as i:
                    for b in range(BANKS):
                        s = out_slot[b % SLOTS]
                        unit = c * per + i * BANKS + (n_resident + b + 1)
                        act.wait_ge(unit_done, unit)
                        act.wait_ge(stored[s], c * (16 * out_per[s]) + i * (16 * BANKS // SLOTS) + 16 * (out_before[s] + b // SLOTS))
                        act.activation(out[:, s], acc[:, (n_resident + b) % BANKS], ACT.Copy).then_inc(evacuated, 1)
                        act.wait_ge(evacuated, unit)
                        dst = featT[bass.ds(i * BANKS + b, 1), :, bass.ds(c * CH, CH)].rearrange("o p t -> p (o t)")
                        act.dma_start(dst, out[:, s]).then_inc(stored[s], 16)
            for s in range(SLOTS):
                act.wait_ge(stored[s], n_chunks * 16 * out_per[s])


def phase_decay(nc, narrowT, w2, L_hi, L_lo):
    with ExitStack() as ctx:
        m = Mem(nc, ctx, "decay")
        B, N2 = 4, 2 * H * GK
        K = 2 * RANK + 1
        glr = m.sb("glr", [K, B, P])
        weights = m.sb("weights", [K, N2])
        mag, expo, log, L = (m.sb(n, [P, B, N2]) for n in ("mag", "expo", "log", "L"))
        hi, lo = (m.sb(n, [P, B, N2], FP32R) for n in ("hi", "lo"))
        logits = m.ps("logits", [P, B, N2])
        weights_in = m.sem("weights_in")
        ones_ready = m.sem("ones_ready")
        glr_in = m.sems("glr_in", B)
        logits_ready = m.sem("logits_ready")
        act_steps = m.sem("act_steps")
        L_ready = m.sem("L_ready")
        hi_ready = m.sem("hi_ready")
        lo_ready = m.sem("lo_ready")
        stored = m.sems("stored", B)
        block = m.block()
        n = TOK // P // B

        @block.sync
        def _(sp):
            sp.dma_start(weights[:, :], w2).then_inc(weights_in, 16)
            with sp.Fori(0, n) as i:
                for b in range(B):
                    sp.wait_ge(logits_ready, i * B)
                    sp.dma_start(glr[0:K - 1, b], narrowT[0:K - 1, bass.ds(i * (B * P) + b * P, P)]).then_inc(glr_in[b], 16)
                for b in range(B):
                    dst = bass.ds(i * (B * P) + b * P, P)
                    sp.wait_ge(lo_ready, i * B + (b + 1))
                    sp.dma_start(L_hi[dst, :], hi[:, b].bitcast(FP32)).then_inc(stored[b], 16)
                    sp.dma_start(L_lo[dst, :], lo[:, b].bitcast(FP32)).then_inc(stored[b], 16)
            for b in range(B):
                sp.wait_ge(stored[b], n * 32)

        @block.tensor
        def _(pe):
            pe.wait_ge(weights_in, 16)
            pe.wait_ge(ones_ready, 1)
            with pe.Fori(0, n) as i:
                for b in range(B):
                    pe.wait_ge(glr_in[b], i * 16 + 16)
                    pe.wait_ge(L_ready, i * B)
                    pe.matmul(logits[:, b], glr[:, b], weights[:, :], start=True, stop=True).then_inc(logits_ready, 1)

        @block.scalar
        def _(act):
            act.preload_act_table_set("natural_log_exp_and_others")
            with act.Fori(0, n) as i:
                for b in range(B):
                    step = Chain(act, act_steps, i * (3 * B) + 3 * b)
                    act.wait_ge(logits_ready, i * B + (b + 1))
                    step(act.activation(mag[:, b], logits[:, b], ACT.Abs))
                    step(act.activation(expo[:, b], mag[:, b], ACT.Exp, scale=-1.0))
                    act.wait_ge(L_ready, i * B)
                    step(act.activation(log[:, b], expo[:, b], ACT.Ln, bias=1.0))

        @block.vector
        def _(dve):
            dve.memset(glr[K - 1:K, :, :], 1.0).then_inc(ones_ready, 1)
            with dve.Fori(0, n) as i:
                for b in range(B):
                    dve.wait_ge(act_steps, i * (3 * B) + (3 * b + 3))
                    dve.wait_ge(stored[b], i * 32)
                    dve.scalar_tensor_tensor(L[:, b], logits[:, b], 0.0, log[:, b], ALU.min, ALU.subtract).then_inc(L_ready, 1)
                    dve.wait_ge(L_ready, i * B + (b + 1))
                    dve.tensor_copy(hi[:, b], L[:, b]).then_inc(hi_ready, 1)
                    dve.wait_ge(hi_ready, i * B + (b + 1))
                    dve.tensor_tensor(lo[:, b], L[:, b], hi[:, b], ALU.subtract).then_inc(lo_ready, 1)


N_TYPES = len(LEVELS) + 2
LAST, INTER = 0, N_TYPES - 1


def gla_matrices():
    sums = np.zeros((2, P, N_TYPES, P), np.float32)
    pairs = np.zeros((2, len(LEVELS), P, P), np.int32)
    s, x = np.meshgrid(np.arange(P), np.arange(P), indexing="ij")
    sums[0, :, LAST], sums[0, :, INTER] = s > x, s <= x
    for n, half in enumerate(LEVELS):
        block, odd = x // half, (x // half) % 2 == 1
        sums[0, :, 1 + n] = np.where(odd, (block * half <= s) & (s <= x), (x < s) & (s < (block + 1) * half))
        pairs[0, n] = odd & (s // half == block - 1)
    sums[1] = sums[0, ::-1, :, ::-1]
    pairs[1] = pairs[0, :, ::-1, ::-1]
    picked = np.zeros((P, 2, len(LEVELS), P // 2), np.int32)
    for d in range(2):
        for n, half in enumerate(LEVELS):
            picked[:, d, n] = pairs[d, n].reshape(P, P // (2 * half), 2, half)[:, :, 1 - d].reshape(P, P // 2)
    return np.ascontiguousarray(sums.transpose(1, 0, 2, 3)), picked


def queries(ap, n, d):
    half = LEVELS[n]
    if len(ap.shape) == 2:
        return ap.rearrange("p (n two m) -> p n two m", two=2, m=half)[:, :, 1 - d, :]
    return ap.rearrange("p h (n two m) -> p h n two m", two=2, m=half)[:, :, :, 1 - d, :]


def phase_gla_forward(nc, featT, L_hi_dram, L_lo_dram, v_dram, sums_dram, picked_dram, diag_dram, ident_dram,
                      o_dram, qb_dram, kb_dram, decb_dram):
    with ExitStack() as ctx:
        m = Mem(nc, ctx, "glaf")
        S, PAIRS, NL = 2, H // 2, len(LEVELS)
        GROUP = 3
        LG = 4
        qk = m.sb("qk", [P, S, 4, P])
        L_hi, L_lo = (m.sb(f"L_{s}", [P, S, 2, PAIRS, P], FP32R) for s in ("hi", "lo"))
        v = m.sb("v", [P, S, H, GV])
        sums_raw = m.sb("sums_raw", [P, 2, N_TYPES * P])
        sums = m.sb("sums", [P, 2, N_TYPES * P], FP32R)
        picked = m.sb("picked", [P, 2, NL, P // 2], I32)
        diag = m.sb("diag", [P, P])
        ident = m.sb("ident", [P, P])
        X = m.sb("X", [P, 2, PAIRS, N_TYPES, P])
        Q = m.sb("Q", [P, 2, PAIRS, N_TYPES - 1, P])
        K = m.sb("K", [P, 2, PAIRS, N_TYPES - 1, P])
        k_tok = m.sb("k_tok", [P, 2, PAIRS, P])
        att = m.sb("att", [P, 2, PAIRS, P])
        o = m.sb("o", [P, S, H * GV])
        state = m.sb("state", [P, PAIRS, GV])
        z_ps = m.ps("z_ps", [P, 3, 512])
        att_ps = m.ps("att_ps", [P, 2, LG, PAIRS, P // 2])
        o_ps = m.ps("o_ps", [P, 2, 512])
        td_ps = m.ps("td_ps", [P, 2, PAIRS, P])
        t_ps, d_ps = td_ps[:, 0], td_ps[:, 1]
        consts_in = m.sem("consts_in")
        loads_started = m.sem("loads_started")
        sums_ready = m.sem("sums_ready")
        qk_in, L_in, v_in = (m.sems(n, S) for n in ("qk_in", "L_in", "v_in"))
        z_done = m.sem("z_done")
        x_ready = m.sem("x_ready")
        mixed = m.sem("mixed")
        pairs_done = m.sem("pairs_done")
        picked_done = m.sem("picked_done")
        picks_started = m.sem("picks_started")
        turned = m.sem("turned")
        k_ready = m.sem("k_ready")
        o_done = m.sem("o_done")
        o_ready = m.sem("o_ready")
        delta_done = m.sem("delta_done")
        state_ready = m.sem("state_ready")
        cleared = m.sem("cleared")
        stored = m.sems("stored", S)
        back_stored = m.sem("back_stored")
        dec = m.sb("dec", [P, PAIRS])
        dec_ready = m.sem("dec_ready")
        block = m.block()
        Z, NGR = 2 * PAIRS, -(-NL // LG)
        PG, PK = 1 + 2 * NGR, 1 + 2 * NL
        TILES = [(0, SEQS[0] // P), (SEQS[0] // P, TOK // P)]

        @block.sync
        def _(sp):
            for dst, src in ((sums_raw, sums_dram), (picked, picked_dram), (diag, diag_dram), (ident, ident_dram)):
                sp.dma_start(dst[tuple(slice(None) for _ in dst.shape)], src).then_inc(consts_in, 16)
            with sp.Fori(0, TOK // P // S) as i:
                for b in range(S):
                    sp.wait_ge(delta_done, i * S)
                    sp.sem_inc(loads_started, 1)
                    tok = bass.ds(i * (S * P) + b * P, P)
                    sp.dma_start(L_hi[:, b].rearrange("p d a c -> p (d a c)").bitcast(FP32), L_hi_dram[tok, :]).then_inc(L_in[b], 16)
                    sp.dma_start(L_lo[:, b].rearrange("p d a c -> p (d a c)").bitcast(FP32), L_lo_dram[tok, :]).then_inc(L_in[b], 16)
                    sp.dma_start(qk[:, b], featT[0:4, :, tok].rearrange("n p t -> p n t")).then_inc(qk_in[b], 16)
                    sp.dma_start(v[:, b].rearrange("p h v -> p (h v)"), v_dram[tok, :]).then_inc(v_in[b], 16)

        @block.tensor
        def _(pe):
            pe.wait_ge(consts_in, 64)
            pe.wait_ge(sums_ready, 1)

            def tile(j, i, b, group):
                pe.wait_ge(L_in[b], i * 32 + 32)
                for d in range(2):
                    for a in range(PAIRS):
                        pe.wait_ge(x_ready, j * Z + (d * PAIRS + a))
                        for g in range(N_TYPES // GROUP):
                            cols = slice(g * GROUP * P, (g + 1) * GROUP * P)
                            for n, half in enumerate((L_hi, L_lo)):
                                done = pe.matmul(z_ps[:, g, 0:GROUP * P], half[:, b, d, a], sums[:, d, cols],
                                                 start=n == 0, stop=n == 1)
                        done.then_inc(z_done, 1)
                pe.wait_ge(qk_in[b], i * 16 + 16)
                pe.wait_ge(picked_done, j * PK)
                for h in range(H):
                    r = slice(GK * (h % 2), GK * (h % 2 + 1))
                    done = pe.matmul(att_ps[:, h % 2, h // 2].rearrange("p a t -> p (a t)"),
                                     qk[r, b, PAIRS + h // 2], qk[r, b, h // 2], start=True, stop=True)
                done.then_inc(pairs_done, 1)
                for d in range(2):
                    pe.wait_ge(mixed, j * Z + (d + 1) * PAIRS)
                    for g in range(NGR):
                        pe.wait_ge(picked_done, j * PK + (1 + d * NL + LG * g))
                        for n in range(LG * g, min(LG * g + LG, NL)):
                            for h in range(H):
                                r = slice(GK * (h % 2), GK * (h % 2 + 1))
                                done = pe.matmul(att_ps[:, h % 2, n % LG, h // 2], K[r, d, h // 2, 1 + n],
                                                 queries(Q[r, d, h // 2, n], n, d), start=True, stop=True)
                        done.then_inc(pairs_done, 1)
                    pe.wait_ge(k_ready, j * 2 + d)
                    pe.wait_ge(state_ready, j)
                    for a in range(PAIRS):
                        done = pe.transpose(t_ps[:, a], K[:, d, a, LAST], ident[:, :])
                    done.then_inc(turned, 1)
                pe.wait_ge(v_in[b], i * 16 + 16)
                pe.wait_ge(picked_done, j * PK + PK)
                pe.wait_ge(cleared, group + 1)
                pe.wait_ge(state_ready, j)
                pe.wait_ge(o_ready, j)
                for h in range(H):
                    r = slice(GK * (h % 2), GK * (h % 2 + 1))
                    cols = slice(h // 2 * GV, (h // 2 + 1) * GV)
                    pe.matmul(o_ps[:, h % 2, cols], att[:, h % 2, h // 2], v[:, b, h], start=True, stop=False)
                    done = pe.matmul(o_ps[:, h % 2, cols], Q[r, 0, h // 2, INTER - 1], state[r, h // 2], start=False, stop=True)
                done.then_inc(o_done, 1)
                pe.wait_ge(k_ready, j * 2 + 2)
                for h in range(H):
                    r = slice(GK * (h % 2), GK * (h % 2 + 1))
                    done = pe.matmul(d_ps[r, h // 2], k_tok[:, 0, h // 2, r], v[:, b, h], start=True, stop=True)
                done.then_inc(delta_done, 1)

            for group, (j0, j1) in enumerate(TILES):
                with pe.Fori(j0 // S, j1 // S) as i:
                    for b in range(S):
                        j = i * S + b
                        tile(j, i, b, group)

        @block.scalar
        def _(act):
            act.preload_act_table(ACT.Exp)
            with act.Fori(0, TOK // P // S) as i:
                for b in range(S):
                    j = i * S + b
                    for d in range(2):
                        for a in range(PAIRS):
                            act.wait_ge(z_done, j * Z + (d * PAIRS + a + 1))
                            if d == 0 and a == 0:
                                act.wait_ge(mixed, j * Z)
                                act.wait_ge(state_ready, j)
                            if d == 1 and a == 0:
                                act.wait_ge(back_stored, j * 48)
                            act.activation(X[:, d, a].rearrange("p (g t) x -> p g (t x)", g=3), z_ps[:, :, 0:GROUP * P], ACT.Exp,
                                           scale=1.0 / TAU).then_inc(x_ready, 1)
                    act.wait_ge(x_ready, j * Z + Z)
                    act.activation(dec[:, :], X[:, 1, :, INTER, 0], ACT.Copy).then_inc(dec_ready, 1)
                    for d in range(2):
                        act.wait_ge(turned, j * 2 + (d + 1))
                        if d == 0:
                            act.wait_ge(delta_done, j)
                        act.activation(k_tok[:, d].rearrange("p a s -> p (a s)"), t_ps.rearrange("p a s -> p (a s)"), ACT.Copy).then_inc(k_ready, 1)
                    act.wait_ge(k_ready, j * 2 + 2)
                    tok = bass.ds(i * (S * P) + b * P, P)
                    act.dma_start(kb_dram[tok, :], k_tok[:, 1].rearrange("p a s -> p (a s)")).then_inc(back_stored, 16)
                    act.wait_ge(mixed, j * Z + Z)
                    act.dma_start(qb_dram[tok, :].rearrange("p (a t) -> p a t", a=PAIRS), Q[:, 1, :, INTER - 1]).then_inc(back_stored, 16)
                    act.wait_ge(dec_ready, j + 1)
                    act.dma_start(decb_dram[tok, :], dec[:, :]).then_inc(back_stored, 16)
                    act.wait_ge(o_done, j + 1)
                    act.wait_ge(stored[b], i * 16)
                    act.activation(o[:, b].rearrange("p (a z v) -> p z a v", z=2, v=GV),
                                   o_ps[:, :, 0:PAIRS * GV].rearrange("p z (a v) -> p z a v", v=GV), ACT.Copy).then_inc(o_ready, 1)
                    act.wait_ge(o_ready, j + 1)
                    act.dma_start(o_dram[tok, :], o[:, b]).then_inc(stored[b], 16)
            for b in range(S):
                act.wait_ge(stored[b], TOK // P // S * 16)
            act.wait_ge(back_stored, TOK // P * 48)

        @block.vector
        def _(dve):
            dve.wait_ge(consts_in, 64)
            dve.tensor_copy(sums[:, :, :], sums_raw[:, :, :]).then_inc(sums_ready, 1)
            for group, (j0, j1) in enumerate(TILES):
                if group:
                    dve.wait_ge(o_done, j0)
                    dve.wait_ge(state_ready, j0)
                dve.memset(state[:, :, :], 0.0).then_inc(cleared, 1)
                dve.wait_ge(cleared, group + 1)
                with dve.Fori(j0 // S, j1 // S) as i:
                    for b in range(S):
                        j = i * S + b
                        dve.wait_ge(qk_in[b], i * 16 + 16)
                        dve.wait_ge(o_done, j)
                        for d in range(2):
                            for a in range(PAIRS):
                                if d == 1 and a == 0:
                                    dve.wait_ge(back_stored, j * 48)
                                dve.wait_ge(x_ready, j * Z + (d * PAIRS + a + 1))
                                shape = [P, N_TYPES - 1, P]
                                dve.tensor_tensor(K[:, d, a], X[:, d, a, 0:N_TYPES - 1],
                                                  qk[:, b, PAIRS + a].unsqueeze(1).broadcast_to(shape), ALU.mult)
                                dve.tensor_tensor(Q[:, d, a], X[:, d, a, 1:N_TYPES],
                                                  qk[:, b, a].unsqueeze(1).broadcast_to(shape), ALU.mult).then_inc(mixed, 1)
                            if d == 0:
                                dve.wait_ge(pairs_done, j * PG + 1)
                                dve.tensor_tensor(att[:, :, :, :], att_ps[:, :, 0:PAIRS].rearrange("p z l a t -> p z l (a t)"),
                                                  diag[:, :].unsqueeze(1).unsqueeze(1).broadcast_to([P, 2, PAIRS, P]), ALU.mult).then_inc(picked_done, 1)
                            for n in range(NL):
                                dve.wait_ge(picked_done, j * PK + (1 + d * NL + n))
                                dve.wait_ge(pairs_done, j * PG + (1 + d * NGR + n // LG + 1))
                                dve.sem_inc(picks_started, 1)
                                half = LEVELS[n]
                                shape = [P, H, P // 2 // half, half]
                                dve.copy_predicated(queries(att[:, :, :, :].rearrange("p z a t -> p (z a) t"), n, d),
                                                    picked[:, d, n].rearrange("p (n m) -> p n m", m=half).unsqueeze(1).broadcast_to(shape),
                                                    att_ps[:, :, n % LG].rearrange("p z a (n m) -> p z a n m", m=half)).then_inc(picked_done, 1)
                        dve.wait_ge(delta_done, j + 1)
                        dve.wait_ge(o_done, j + 1)
                        for a in range(PAIRS):
                            done = dve.scalar_tensor_tensor(state[:, a], state[:, a], X[:, 0, a, INTER, P - 1:P], d_ps[:, a], ALU.mult, ALU.add)
                        done.then_inc(state_ready, 1)


def phase_gla_backward(nc, v_dram, o_dram, qb_dram, kb_dram, decb_dram, gain_dram, ident_dram, oT):
    with ExitStack() as ctx:
        m = Mem(nc, ctx, "glab")
        S, PAIRS = 2, H // 2
        qb = m.sb("qb", [P, S, PAIRS, P])
        kb = m.sb("kb", [P, S, PAIRS, P])
        dec = m.sb("dec", [P, S, PAIRS])
        v = m.sb("v", [P, S, H, GV])
        o = m.sb("o", [P, S, H * GV])
        total = m.sb("total", [P, H, GV])
        sq = m.sb("sq", [P, H, GV])
        normed_o = m.sb("normed_o", [P, S, H, GV])
        gain = m.sb("gain", [P, GV])
        ident = m.sb("ident", [P, P])
        stat = m.sb("stat", [P, 4, H])
        state = m.sb("state", [P, PAIRS, GV])
        out = m.sb("out", [P, S, H, P])
        o_ps = m.ps("o_ps", [P, S, 2, 512])
        d_ps = m.ps("d_ps", [P, S, 512])
        t_ps = m.ps("t_ps", [P, S, H, P])
        consts_in = m.sem("consts_in")
        tile_in = m.sems("tile_in", S)
        loads_started = m.sem("loads_started")
        o_done = m.sem("o_done")
        delta_done = m.sem("delta_done")
        cleared = m.sem("cleared")
        state_ready = m.sem("state_ready")
        steps = m.sem("steps")
        normed = m.sem("normed")
        turned = m.sem("turned")
        copied = m.sem("copied")
        stored = m.sems("stored", S)
        block = m.block()
        STEPS = 4 + RSQRT_STEPS
        GROUPS = [(0, SEQS[0] // P, 0), (SEQS[0] // P, TOK // P, SEQS[0])]

        def groups(engine, body):
            for group, (j0, j1, first) in enumerate(GROUPS):
                with engine.Fori(0, (j1 - j0) // S) as i:
                    for b in range(S):
                        t0 = engine.snap((first + (j1 - j0 - 1 - b) * P) - i * (S * P))
                        body(i * S + (j0 + b), i + j0 // S, b, group, t0)

        @block.sync
        def _(sp):
            sp.dma_start(gain[:, :], gain_dram).then_inc(consts_in, 16)
            sp.dma_start(ident[:, :], ident_dram).then_inc(consts_in, 16)

            def load(n, i, b, group, t0):
                sp.wait_ge(normed, i * S)
                sp.wait_ge(state_ready, i * S)
                sp.sem_inc(loads_started, 1)
                tok = bass.ds(t0, P)
                sp.dma_start(qb[:, b].rearrange("p a t -> p (a t)"), qb_dram[tok, :]).then_inc(tile_in[b], 16)
                sp.dma_start(kb[:, b].rearrange("p a t -> p (a t)"), kb_dram[tok, :]).then_inc(tile_in[b], 16)
                sp.dma_start(dec[:, b], decb_dram[tok, :]).then_inc(tile_in[b], 16)
                sp.dma_start(v[:, b].rearrange("p h v -> p (h v)"), v_dram[tok, :]).then_inc(tile_in[b], 16)
                sp.dma_start(o[:, b], o_dram[tok, :]).then_inc(tile_in[b], 16)
            groups(sp, load)

        @block.tensor
        def _(pe):
            pe.wait_ge(consts_in, 32)

            def tile(n, i, b, group, t0):
                pe.wait_ge(tile_in[b], i * 80 + 80)
                pe.wait_ge(cleared, group + 1)
                pe.wait_ge(state_ready, n)
                pe.wait_ge(normed, i * S)
                for h in range(H):
                    r = slice(GK * (h % 2), GK * (h % 2 + 1))
                    done = pe.matmul(o_ps[:, b, h % 2, h // 2 * GV:(h // 2 + 1) * GV], qb[r, b, h // 2], state[r, h // 2], start=True, stop=True)
                done.then_inc(o_done, 1)
                for h in range(H):
                    r = slice(GK * (h % 2), GK * (h % 2 + 1))
                    done = pe.matmul(d_ps[r, b, (h // 2) * GV:(h // 2 + 1) * GV], kb[:, b, h // 2, r], v[:, b, h], start=True, stop=True)
                done.then_inc(delta_done, 1)
                pe.wait_ge(normed, n + 1)
                pe.wait_ge(copied, i * S)
                for h in range(H):
                    done = pe.transpose(t_ps[:, b, h], normed_o[:, b, h], ident[:, :])
                done.then_inc(turned, 1)
            groups(pe, tile)

        @block.vector
        def _(dve):
            dve.wait_ge(consts_in, 32)
            dve.tensor_scalar(gain[:, :], gain[:, :], GK ** -0.5, None, ALU.mult).then_inc(steps, 1)

            def tile(n, i, b, group, t0):
                dve.wait_ge(o_done, n + 1)
                dve.wait_ge(delta_done, n + 1)
                for a in range(PAIRS):
                    done = dve.scalar_tensor_tensor(state[:, a], state[:, a], dec[:, b, a:a + 1], d_ps[:, b, a * GV:(a + 1) * GV], ALU.mult, ALU.add)
                done.then_inc(state_ready, 1)
                dve.wait_ge(normed, n)
                step = Chain(dve, steps, n * STEPS + 1)
                step(dve.tensor_tensor(total[:, :, :].rearrange("p (a z) v -> p z a v", z=2),
                                       o_ps[:, b, :, 0:PAIRS * GV].rearrange("p z (a v) -> p z a v", v=GV),
                                       o[:, b].rearrange("p (a z v) -> p z a v", z=2, v=GV), ALU.add))
                step(dve.tensor_tensor(sq[:, :, :], total[:, :, :], total[:, :, :], ALU.mult))
                step(dve.tensor_reduce(stat[:, 0], sq[:, :, :], AXX, ALU.add))
                step(dve.tensor_scalar(stat[:, 1], stat[:, 0], 1.0 / GV / GK, EPS, ALU.mult, ALU.add))
                rsqrt(step, dve, stat[:, 2], stat[:, 1], stat[:, 3])
                dve.wait_ge(turned, i * S)
                for h in range(H):
                    done = dve.scalar_tensor_tensor(normed_o[:, b, h], total[:, h], stat[:, 2, h:h + 1], gain[:, :], ALU.mult, ALU.mult)
                done.then_inc(normed, 1)

            for group, (j0, j1, first) in enumerate(GROUPS):
                if group:
                    dve.wait_ge(o_done, j0)
                    dve.wait_ge(state_ready, j0)
                dve.memset(state[:, :, :], 0.0).then_inc(cleared, 1)
                dve.wait_ge(cleared, group + 1)
                with dve.Fori(0, (j1 - j0) // S) as i:
                    for b in range(S):
                        tile(i * S + (j0 + b), i + j0 // S, b, group, None)

        @block.scalar
        def _(act):
            act.preload_act_table(ACT.Exp)

            def tile(n, i, b, group, t0):
                act.wait_ge(turned, n + 1)
                act.wait_ge(stored[b], i * 16)
                act.activation(out[:, b].rearrange("p h t -> p (h t)"), t_ps[:, b].rearrange("p h t -> p (h t)"), ACT.Copy).then_inc(copied, 1)
                act.wait_ge(copied, n + 1)
                act.dma_start(oT[0:H, :, bass.ds(t0, P)].rearrange("h p t -> p h t"), out[:, b]).then_inc(stored[b], 16)
            groups(act, tile)
            for b in range(S):
                act.wait_ge(stored[b], TOK // P // S * 16)


def phase_diff(nc, name, featT, v_dram, first, T, alibi_dram, slopes_dram, lambda_dram, ident_dram, o_dram):
    with ExitStack() as ctx:
        m = Mem(nc, ctx, name)
        S, HD, G, LAG = 2, 64, 4, 5
        nq, half = T // P, min(T, 1024)
        halves, KU = T // half, T // P // G
        SH = 2 * halves
        HB = 2 * G // nq if nq < 2 * G else 1
        U, BODIES = HB * nq, H // HB
        k_raw = m.sb("k_raw", [P, 2, T])
        k_hi, k_lo = (m.sb(f"k_{s}", [P, 2, T], FP32R) for s in ("hi", "lo"))
        v_raw = m.sb("v_raw", [P, nq, P])
        v_hi, v_lo = (m.sb(f"v_{s}", [P, nq, P], FP32R) for s in ("hi", "lo"))
        q_raw = m.sb("q_raw", [P, S, 2, P])
        q = m.sb("q", [P, S, 2, P], FP32R)
        table = m.sb("table", [P, 2 * T - P])
        p = m.sb("p", [P, S, 2, T])
        a = m.sb("a", [P, 2, G, T])
        aT_hi, aT_lo = (m.sb(f"aT_{s}", [P, 2, G * P], FP32R) for s in ("hi", "lo"))
        outT = m.sb("outT", [P, G * P])
        o = m.sb("o", [P, 2, G, P])
        slopes = m.sb("slopes", [P, H + 2, 3])
        lam_in = m.sb("lam_in", [P, 2, 2, HD])
        lam_products = m.sb("lam_products", [P, 2, HD])
        lam = m.sb("lam", [P, 6])
        ident = m.sb("ident", [P, P])
        stat = m.sb("stat", [P, S, 10])
        MAX, NEG_MAX, SUM, RATIO = 0, 4, 6, 8
        parts = m.sb("parts", [P, S, 2, 2])
        inverse = m.sb("inverse", [P, 2, G, 2])
        inverse_out = m.sb("inverse_out", [P, G])
        s_ps = m.ps("s_ps", [P, 2, 1024])
        t_ps = m.ps("t_ps", [P, 2, G * P])
        oT_ps = m.ps("oT_ps", [P, G * P])
        o_ps = m.ps("o_ps", [P, G, P])
        consts_in = m.sem("consts_in")
        cleared = m.sem("cleared")
        k_in, k_hi_ready, k_ready = (m.sem(f"k_{s}") for s in ("in", "hi_ready", "ready"))
        v_in, v_hi_ready, v_ready = (m.sem(f"v_{s}") for s in ("in", "hi_ready", "ready"))
        q_in = m.sems("q_in", S)
        q_scaled = m.sem("q_scaled")
        q_ready = m.sem("q_ready")
        scores_done = m.sem("scores_done")
        biased = m.sem("biased")
        max_ready = m.sem("max_ready")
        p_ready = m.sem("p_ready")
        ratio_steps = m.sem("ratio_steps")
        lam_steps = m.sem("lam_steps")
        lam_exp = m.sem("lam_exp")
        combined = m.sem("combined")
        far_scaled = m.sem("far_scaled")
        far_combined = m.sem("far_combined")
        turned = m.sem("turned")
        hi_ready = m.sem("hi_ready")
        lo_ready = m.sem("lo_ready")
        turn_used = m.sem("turn_used")
        outT_ready = m.sem("outT_ready")
        inverse_taken = m.sem("inverse_taken")
        turned_back = m.sem("turned_back")
        scaled = m.sem("scaled")
        stored = m.sems("stored", 2)
        sp_passed, act_passed, dve_passed, pool_passed = (m.sem(f"{e}_passed") for e in ("sp", "act", "dve", "pool"))
        SCORES0, BIASED0, Q0, TURNED0, LO0, USED0, COMBINED0 = SH, 2, 1, 3 * KU, 1, 1, 3
        split_units = [u for u in range(U) if (u - LAG) % nq == 0]
        near, far = slice(0, T // 2), slice(T // 2, T)
        block = m.block()

        class Unit:

            def __init__(self, c, u):
                self.u, self.n, self.h, self.tile = u, c * U + u, c * HB + u // nq, u % nq
                self.slot, self.turn = u % S, c * (U // S) + u // S
                self.next_h = c * HB + (u + 1) // nq
                self.old_free = c * (U * KU) + (KU * (G * ((u - 1) // G) + 1) + TURNED0)
                self.old_h, self.old_slot, self.old, self.old_group = c * HB + (u - 1) // nq, (u - 1) % S, (u - 1) % G, (u - 1) // G % 2
                self.quarter, self.group = (u - LAG) % G, (u - LAG) // G % 2
                self.group_combined = c * U + G * ((u - LAG) // G) + G + 1 + COMBINED0
                self.out = c * (U // G) + (u - 1) // G
                self.out_slot, self.out_turn = (u - 1) // G % 2, c * (U // G // 2) + (u - 1) // G // 2
                self.starts_out, self.ends_out = u % G == 1, u % G == 0
                self.splits_v = (u - LAG) % nq == 0
                self.v_splits = c * HB + 1 + sum(s <= u for s in split_units)
                self.v_head = c * HB + (u - LAG) // nq
                self.s = self.n * KU
                self.e = self.n * SH

        def turns(engine, body):
            with engine.Fori(0, BODIES) as c:
                for u in range(U):
                    body(Unit(c, u), True)
            for u in range(LAG):
                body(Unit(BODIES, u), False)

        def slot(u, c):
            return (u.u * KU + c) % 2

        def one(ap, i):
            return ap[:, bass.ds(i, 1), :].rearrange("p o c -> p (o c)")

        def keys(b):
            return b // halves, slice(b % halves * half, (b % halves + 1) * half)

        @block.sync
        def _(sp):
            for dst, src in ((table[:, :], alibi_dram[:, ALIBI_MID - (T - P):ALIBI_MID + T]), (slopes[:, :, :], slopes_dram),
                             (lam_in[:, :, :, :], lambda_dram), (ident[:, :], ident_dram)):
                sp.dma_start(dst, src).then_inc(consts_in, 16)

            def load_v(h):
                if h:
                    sp.wait_ge(v_ready, h + (1 if nq > LAG else 2))
                sp.dma_start(v_raw[:, :, :], v_dram[first:first + T, h * P:(h + 1) * P].rearrange("(n p) v -> p n v", p=P)).then_inc(v_in, 16)

            for h in range(H):
                if h:
                    sp.wait_ge(k_ready, h * SH)
                src = featT[DK_BLOCK + h, :, first:first + T].rearrange("(i d) t -> d i t", i=2)
                for r in (slice(0, HD), slice(HD, P)):
                    sp.dma_start(k_raw[r], src).then_inc(k_in, 16)
                if h == 0 or nq > LAG:
                    load_v(h)
                with sp.Fori(0, nq // S) as i:
                    for b in range(S):
                        sp.wait_ge(q_ready, i * S + (h * nq + b - 1 + Q0))
                        sp.sem_inc(sp_passed, 1)
                        src = featT[DQ_BLOCK + h, :, bass.ds(i * (S * P) + (b * P + first), P)].rearrange("(i d) t -> d i t", i=2)
                        for r in (slice(0, HD), slice(HD, P)):
                            sp.dma_start(q_raw[r, b], src).then_inc(q_in[b], 16)
                if h and nq <= LAG:
                    load_v(h)
            sp.wait_ge(q_ready, H * nq - 1 + Q0)
            for r in (slice(0, HD), slice(HD, P)):
                sp.dma_start(q_raw[r, 0], featT[DQ_BLOCK, :, first:first + P].rearrange("(i d) t -> d i t", i=2)).then_inc(q_in[0], 16)

        @block.gpsimd
        def _(pool):
            pool.sem_inc(q_ready, Q0)
            pool.sem_inc(far_combined, COMBINED0)
            pool.memset(a[:, 1], 0.0).then_inc(cleared, 1)
            pool.wait_ge(cleared, 3)

            def query_low(n, b):
                pool.wait_ge(q_scaled, n * 2 + 2)
                pool.sem_inc(pool_passed, 1)
                pool.tensor_tensor(q[HD:P, b], q_raw[HD:P, b], q[HD:P, b], ALU.subtract).then_inc(q_ready, 1)
                pool.wait_ge(q_ready, n + (1 + Q0))
                pool.sem_inc(pool_passed, 1)

            query_low(0, 0)

            def turn(u, has_scores):
                if has_scores:
                    query_low(u.n + 1, (u.u + 1) % S)
                elif u.u:
                    return
                pool.wait_ge(far_scaled, u.n + 1)
                pool.wait_ge(turned, u.old_free)
                pool.sem_inc(pool_passed, 1)
                pool.tensor_tensor(a[:, u.old_group, u.old, far], p[:, u.old_slot, 1, far], p[:, u.old_slot, 0, far], ALU.add).then_inc(far_combined, 1)
                pool.wait_ge(far_combined, u.n + (1 + COMBINED0))
                pool.sem_inc(pool_passed, 1)
            turns(pool, turn)

        @block.tensor
        def _(pe):
            pe.sem_inc(scores_done, SCORES0)
            pe.sem_inc(turned, TURNED0)
            pe.sem_inc(turn_used, USED0)
            pe.wait_ge(consts_in, 64)
            pe.wait_ge(cleared, 3)
            pe.matmul(oT_ps[:, :], ident[:, :], a[:, 0, 0, 0:G * P], start=True, stop=False)

            def scores(u, b):
                i, cols = keys(b)
                if b == 0:
                    pe.wait_ge(q_ready, u.n + (1 + Q0))
                if u.tile == 0:
                    pe.wait_ge(k_ready, u.h * SH + (b + 1))
                pe.wait_ge(biased, u.e + (b - 1 + BIASED0))
                for c in range(half // 512):
                    for n, part in enumerate((k_hi, k_lo)):
                        done = pe.matmul(s_ps[:, b % 2, c * 512:(c + 1) * 512], q[:, u.slot, i],
                                         part[:, i, cols.start + c * 512:cols.start + (c + 1) * 512], start=n == 0, stop=n == 1)
                done.then_inc(scores_done, 1)

            def transposes(u, c):
                if c == 0:
                    pe.wait_ge(combined, u.group_combined)
                    pe.wait_ge(far_combined, u.group_combined)
                pe.wait_ge(lo_ready, u.s + (c - 1 + LO0))
                kt = u.quarter * KU + c
                for j in range(G):
                    done = pe.transpose(t_ps[:, slot(u, c), j * P:(j + 1) * P], a[:, u.group, j, kt * P:(kt + 1) * P], ident[:, :])
                done.then_inc(turned, 1)

            def values(u, c):
                if c == 0:
                    pe.wait_ge(v_ready, u.v_splits)
                    if u.starts_out:
                        pe.wait_ge(outT_ready, u.out + 1)
                pe.wait_ge(lo_ready, u.s + (c + 1 + LO0))
                kt, s = u.quarter * KU + c, slot(u, c)
                product3(pe, oT_ps[:, :], v_hi[:, kt], v_lo[:, kt], aT_hi[:, s], aT_lo[:, s], kt == 0, kt == nq - 1).then_inc(turn_used, 1)

            def turn_back(u):
                pe.wait_ge(outT_ready, u.out + 1)
                pe.wait_ge(scaled, u.out)
                for j in range(G):
                    done = pe.transpose(o_ps[:, j], outT[:, j * P:(j + 1) * P], ident[:, :])
                done.then_inc(turned_back, 1)

            def turn(u, has_scores):
                def score(b):
                    if has_scores and b < SH:
                        scores(u, b)
                transposes(u, 0)
                score(0)
                if KU > 1:
                    transposes(u, 1)
                score(1)
                if u.starts_out:
                    turn_back(u)
                for c in range(KU):
                    values(u, c)
                    if c + 2 < KU:
                        transposes(u, c + 2)
                        score(c + 2)
            turns(pe, turn)
            turn_back(Unit(BODIES, LAG))

        @block.scalar
        def _(act):
            act.preload_act_table(ACT.Exp)
            act.wait_ge(lam_steps, 2)
            act.activation(lam[:, 2:4], lam[:, 0:2], ACT.Exp).then_inc(lam_exp, 1)
            act.wait_ge(v_in, 16)
            act.activation(v_hi[:, :, :], v_raw[:, :, :], ACT.Copy).then_inc(v_hi_ready, 1)
            act.wait_ge(cleared, 3)
            act.wait_ge(consts_in, 64)

            def high(u, c):
                act.wait_ge(turned, u.s + (c + 1 + TURNED0))
                act.wait_ge(turn_used, u.s + (c - 1 + USED0))
                act.activation(aT_hi[:, slot(u, c)], t_ps[:, slot(u, c)], ACT.Copy).then_inc(hi_ready, 1)

            def exponentials(u, b):
                i, cols = keys(b)
                s, h = (u.old_slot, u.old_h) if i else (u.slot, u.h)
                act.wait_ge(max_ready, u.n * 2 + (1 - i))
                act.sem_inc(act_passed, 1)
                act.activation(p[:, s, i, cols], p[:, s, i, cols], ACT.Exp, bias=stat[:, s, NEG_MAX + i:NEG_MAX + i + 1],
                               scale=one(slopes, h + 1)[:, 1:2], accum_out=parts[:, s, i, b % halves:b % halves + 1]).then_inc(p_ready, 1)

            def queries_of(n, h, b, turn, scores):
                act.wait_ge(q_in[b], turn * 32 + 32)
                act.wait_ge(scores_done, scores)
                act.sem_inc(act_passed, 1)
                act.activation(q[:, b], q_raw[:, b], ACT.Identity, scale=one(slopes, h + 1)[:, 0:1]).then_inc(q_scaled, 1)
                act.wait_ge(q_scaled, n * 2 + 1)
                act.sem_inc(act_passed, 1)
                act.activation(q_raw[:, b], q_raw[:, b], ACT.Identity, scale=one(slopes, h + 1)[:, 0:1]).then_inc(q_scaled, 1)

            def scale_far(u):
                act.wait_ge(ratio_steps, u.n * 3 + 3)
                act.activation(p[:, u.old_slot, 1, far], p[:, u.old_slot, 1, far], ACT.Identity,
                               scale=stat[:, u.old_slot, RATIO:RATIO + 1]).then_inc(far_scaled, 1)

            def take_output(u):
                act.wait_ge(turn_used, u.s + USED0)
                act.wait_ge(turned_back, u.out)
                act.activation(outT[:, :], oT_ps[:, :], ACT.Copy).then_inc(outT_ready, 1)
                act.wait_ge(scaled, u.out)
                act.activation(inverse_out[:, :], inverse[:, u.out_slot, :, 0], ACT.Copy).then_inc(inverse_taken, 1)

            def scale_output(u):
                act.wait_ge(turned_back, u.out + 1)
                act.wait_ge(inverse_taken, u.out + 1)
                act.wait_ge(stored[u.out_slot], u.out_turn * 16)
                for j in range(G):
                    done = act.activation(o[:, u.out_slot, j], o_ps[:, j], ACT.Identity, scale=inverse_out[:, j:j + 1])
                done.then_inc(scaled, 1)
                act.wait_ge(scaled, u.out + 1)
                act.dma_start(o_dram[bass.ds(u.out * (G * P), G * P), :].rearrange("(j p) v -> p j v", p=P), o[:, u.out_slot]).then_inc(stored[u.out_slot], 16)

            def turn(u, has_scores):
                if has_scores and u.tile == 0:
                    act.wait_ge(k_in, u.h * 32 + 32)
                    act.wait_ge(scores_done, u.e + SCORES0)
                    for b in range(SH):
                        i, cols = keys(b)
                        act.activation(k_hi[:, i, cols], k_raw[:, i, cols], ACT.Copy).then_inc(k_hi_ready, 1)
                if u.splits_v:
                    act.wait_ge(v_in, u.v_head * 16 + 16)
                    act.wait_ge(turn_used, u.s + USED0)
                    act.activation(v_hi[:, :, :], v_raw[:, :, :], ACT.Copy).then_inc(v_hi_ready, 1)
                if u.starts_out:
                    take_output(u)
                later = has_scores or u.u == 0
                high(u, 0)
                if later:
                    exponentials(u, halves)
                if KU > 1:
                    high(u, 1)
                if has_scores:
                    queries_of(u.n + 1, u.next_h, (u.u + 1) % S, u.turn + u.u % S, u.e + SCORES0)
                if later and halves > 1:
                    exponentials(u, halves + 1)
                for c in range(2, max(KU, halves + 2)):
                    if c < KU:
                        high(u, c)
                    if c == max(KU, halves + 2) - 1 and later:
                        scale_far(u)
                    if has_scores and c - 2 < halves:
                        exponentials(u, c - 2)
                if u.starts_out:
                    scale_output(u)
            queries_of(0, 0, 0, 0, SCORES0)
            turns(act, turn)
            last = Unit(BODIES, LAG)
            take_output(last)
            scale_output(last)
            n_out = BODIES * (U // G) + 2
            for b in range(2):
                act.wait_ge(stored[b], n_out // 2 * 16)

        @block.vector
        def _(dve):
            dve.sem_inc(biased, BIASED0)
            dve.sem_inc(combined, COMBINED0)
            dve.sem_inc(lo_ready, LO0)
            dve.memset(a[:, 0], 0.0).then_inc(cleared, 1)
            dve.memset(p[:, :, :, :], 0.0)
            dve.memset(inverse[:, :, :, :], 1.0)
            dve.memset(parts[:, :, :, 0:1], 1.0)
            dve.memset(parts[:, :, :, 1:2], 0.0)
            dve.memset(stat[:, :, :], 1.0).then_inc(cleared, 1)
            dve.wait_ge(cleared, 3)
            dve.wait_ge(consts_in, 64)
            step = Chain(dve, lam_steps)
            step(dve.tensor_tensor(lam_products[:, :, :], lam_in[:, :, 0], lam_in[:, :, 1], ALU.mult))
            step(dve.tensor_reduce(lam[:, 0:2], lam_products[:, :, :], AXX, ALU.add))
            dve.wait_ge(lam_exp, 1)
            step(dve.tensor_tensor(lam[:, 4:5], lam[:, 3:4], lam[:, 2:3], ALU.subtract))
            step(dve.tensor_scalar(lam[:, 5:6], lam[:, 4:5], 1.0, -LAMBDA_INIT, ALU.mult, ALU.add))
            dve.wait_ge(v_hi_ready, 1)
            dve.tensor_tensor(v_lo[:, :, :], v_raw[:, :, :], v_hi[:, :, :], ALU.subtract).then_inc(v_ready, 1)

            def bias_max(u, b):
                i, cols = keys(b)
                f, start = b % halves, T - P - u.tile * P
                if b == 0:
                    dve.wait_ge(combined, u.n + COMBINED0)
                if b == halves - 1:
                    dve.wait_ge(far_combined, u.n + COMBINED0)
                if f:
                    dve.wait_ge(biased, u.e + (b + BIASED0))
                dve.wait_ge(scores_done, u.e + (b + 1 + SCORES0))
                dve.sem_inc(dve_passed, 1)
                at = MAX + 2 * i + f
                dve.tensor_tensor_reduce(out=p[:, u.slot, i, cols], in0=s_ps[:, b % 2, 0:half], in1=table[:, start + cols.start:start + cols.stop],
                                         scale=1.0, scalar=stat[:, u.slot, at - 1:at] if f else -3.0e38, op0=ALU.add, op1=ALU.max,
                                         accum_out=stat[:, u.slot, at:at + 1]).then_inc(biased, 1)
                if f == halves - 1:
                    dve.wait_ge(biased, u.e + (b + 1 + BIASED0))
                    dve.tensor_scalar(stat[:, u.slot, NEG_MAX + i:NEG_MAX + i + 1], stat[:, u.slot, at:at + 1],
                                      one(slopes, u.h + 1)[:, 2:3], None, ALU.mult).then_inc(max_ready, 1)

            def ratio(u):
                b, j, g = u.old_slot, u.old, u.old_group
                dve.wait_ge(p_ready, u.e + SH // 2)
                if u.starts_out:
                    dve.wait_ge(inverse_taken, u.out + 1)
                step = Chain(dve, ratio_steps, u.n * 3)
                step(dve.tensor_tensor(stat[:, b, SUM:SUM + 2].unsqueeze(2), parts[:, b, :, 0:1], parts[:, b, :, 1:2], ALU.add))
                step(dve.reciprocal(inverse[:, g, j], stat[:, b, SUM:SUM + 2]))
                step(dve.tensor_scalar(stat[:, b, RATIO:RATIO + 1], inverse[:, g, j, 1:2], stat[:, b, SUM:SUM + 1],
                                       lam[:, 5:6], ALU.mult, ALU.mult))

            def low(u, c):
                dve.wait_ge(hi_ready, u.s + (c + 1))
                dve.tensor_tensor(aT_lo[:, slot(u, c)], t_ps[:, slot(u, c)], aT_hi[:, slot(u, c)], ALU.subtract).then_inc(lo_ready, 1)

            def combine(u):
                dve.wait_ge(turned, u.old_free)
                dve.sem_inc(dve_passed, 1)
                dve.scalar_tensor_tensor(a[:, u.old_group, u.old, near], p[:, u.old_slot, 1, near], stat[:, u.old_slot, RATIO:RATIO + 1],
                                         p[:, u.old_slot, 0, near], ALU.mult, ALU.add).then_inc(combined, 1)

            def turn(u, has_scores):
                if has_scores and u.tile == 0:
                    for b in range(SH):
                        i, cols = keys(b)
                        dve.wait_ge(k_hi_ready, u.h * SH + (b + 1))
                        dve.tensor_tensor(k_lo[:, i, cols], k_raw[:, i, cols], k_hi[:, i, cols], ALU.subtract).then_inc(k_ready, 1)
                if u.splits_v:
                    dve.wait_ge(v_hi_ready, u.v_splits)
                    dve.tensor_tensor(v_lo[:, :, :], v_raw[:, :, :], v_hi[:, :, :], ALU.subtract).then_inc(v_ready, 1)
                for b in range(SH):
                    if has_scores:
                        bias_max(u, b)
                    if b == SH - 2 and (has_scores or u.u == 0):
                        ratio(u)
                    if b < KU:
                        low(u, b)
                if has_scores or u.u == 0:
                    combine(u)
            turns(dve, turn)


def phase_cross(nc, featT, kT_dram, v_dram, ident_dram, o_dram):
    with ExitStack() as ctx:
        m = Mem(nc, ctx, "cross")
        S, HD = 2, P
        MT = N_MEM // P
        SCALE = HD ** -0.5
        kT = m.sb("kT", [P, 2, H, N_MEM])
        v = m.sb("v", [P, 2, MT, H * HD])
        q = m.sb("q", [P, S, H, P])
        p = m.sb("p", [P, S, H, N_MEM])
        pT = m.sb("pT", [P, S, MT, H, P])
        o = m.sb("o", [P, S, H, HD])
        ident = m.sb("ident", [P, P])
        stat = m.sb("stat", [P, S, 4, H])
        MAX, NEG_MAX, SUM, RSUM = range(4)
        s_ps = m.ps("s_ps", [P, H, N_MEM])
        t_ps = m.ps("t_ps", [P, 2, 2, 512])
        o_ps = m.ps("o_ps", [P, S, H, HD])
        consts_in = m.sem("consts_in")
        q_in = m.sems("q_in", S)
        scores_done = m.sem("scores_done")
        stat_steps = m.sem("stat_steps")
        max_ready = m.sem("max_ready")
        p_ready = m.sem("p_ready")
        sums_inverted = m.sem("sums_inverted")
        turned = m.sem("turned")
        pT_ready = m.sem("pT_ready")
        pv_done = m.sem("pv_done")
        scaled = m.sem("scaled")
        stored = m.sems("stored", S)
        block = m.block()
        GROUPS = [(g, j0 // S, j1 // S) for g, (j0, j1) in enumerate([(0, SEQS[0] // P), (SEQS[0] // P, TOK // P)])]

        def tiles(engine, body):
            for g, i0, i1 in GROUPS:
                with engine.Fori(i0, i1) as i:
                    for b in range(S):
                        body(i * S + b, i, b, g)

        @block.sync
        def _(sp):
            sp.dma_start(ident[:, :], ident_dram).then_inc(consts_in, 16)
            for g in range(2):
                rows_of = slice(g * N_MEM, (g + 1) * N_MEM)
                sp.dma_start(kT[:, g], kT_dram[:, :, rows_of].rearrange("h p s -> p h s")).then_inc(consts_in, 16)
                sp.dma_start(v[:, g], v_dram[rows_of, :].rearrange("(n p) v -> p n v", p=P)).then_inc(consts_in, 16)

            def load(n, i, b, g):
                sp.wait_ge(scores_done, i * S)
                sp.dma_start(q[:, b], featT[CQ_BLOCK:CQ_BLOCK + H, :, bass.ds(n * P, P)].rearrange("h p t -> p h t")).then_inc(q_in[b], 16)
            tiles(sp, load)

        @block.tensor
        def _(pe):
            pe.wait_ge(consts_in, 16 * 5)

            def tile(n, i, b, g):
                pe.wait_ge(q_in[b], i * 16 + 16)
                pe.wait_ge(p_ready, n)
                for h in range(H):
                    done = pe.matmul(s_ps[:, h], q[:, b, h], kT[:, g, h], start=True, stop=True)
                done.then_inc(scores_done, 1)
                pe.wait_ge(p_ready, n + 1)
                pe.wait_ge(pT_ready, i * (2 * S))
                for k in range(MT):
                    for h in range(H):
                        done = pe.transpose(t_ps[:, b, k, h * P:(h + 1) * P], p[:, b, h, k * P:(k + 1) * P], ident[:, :])
                    done.then_inc(turned, 1)
                pe.wait_ge(pT_ready, n * 2 + 2)
                pe.wait_ge(scaled, i * S)
                for h in range(H):
                    for k in range(MT):
                        done = pe.matmul(o_ps[:, b, h], pT[:, b, k, h], v[:, g, k, h * HD:(h + 1) * HD], start=k == 0, stop=k == MT - 1)
                done.then_inc(pv_done, 1)
            tiles(pe, tile)

        @block.scalar
        def _(act):
            act.preload_act_table(ACT.Exp)

            def tile(n, i, b, g):
                act.wait_ge(max_ready, n + 1)
                act.wait_ge(turned, i * (2 * S))
                for h in range(H):
                    done = act.activation(p[:, b, h], s_ps[:, h], ACT.Exp, bias=stat[:, b, NEG_MAX, h:h + 1], scale=SCALE,
                                          accum_out=stat[:, b, SUM, h:h + 1])
                done.then_inc(p_ready, 1)
                act.wait_ge(pv_done, n + 1)
                act.wait_ge(sums_inverted, n + 1)
                act.wait_ge(stored[b], i * 16)
                for h in range(H):
                    done = act.activation(o[:, b, h], o_ps[:, b, h], ACT.Identity, scale=stat[:, b, RSUM, h:h + 1])
                done.then_inc(scaled, 1)
                act.wait_ge(scaled, n + 1)
                act.dma_start(o_dram[bass.ds(n * P, P), :], o[:, b].rearrange("p h v -> p (h v)")).then_inc(stored[b], 16)
            tiles(act, tile)
            for b in range(S):
                act.wait_ge(stored[b], TOK // P // S * 16)

        @block.vector
        def _(dve):
            def tile(n, i, b, g):
                dve.wait_ge(scores_done, n + 1)
                dve.wait_ge(scaled, i * S)
                dve.tensor_reduce(stat[:, b, MAX], s_ps[:, :, :], AXX, ALU.max).then_inc(stat_steps, 1)
                dve.wait_ge(stat_steps, n + 1)
                dve.tensor_scalar(stat[:, b, NEG_MAX], stat[:, b, MAX], -SCALE, None, ALU.mult).then_inc(max_ready, 1)
                dve.wait_ge(p_ready, n + 1)
                dve.reciprocal(stat[:, b, RSUM], stat[:, b, SUM]).then_inc(sums_inverted, 1)
                dve.wait_ge(pv_done, i * S)
                for k in range(MT):
                    dve.wait_ge(turned, n * 2 + (k + 1))
                    dve.tensor_copy(pT[:, b, k].rearrange("p h t -> p (h t)"), t_ps[:, b, k]).then_inc(pT_ready, 1)
            tiles(dve, tile)


def phase_heads(nc, diff_o, cross_o, gains_dram, ident_dram, oT):
    with ExitStack() as ctx:
        m = Mem(nc, ctx, "heads")
        S, NO = 2, 2
        o = m.sb("o", [P, S, NO, H, P])
        sq = m.sb("sq", [P, H, P])
        gain = m.sb("gain", [P, P])
        ident = m.sb("ident", [P, P])
        stat = m.sb("stat", [P, 4, H])
        out = m.sb("out", [P, S, NO, H * P])
        t_ps = m.ps("t_ps", [P, S, NO, H * P])
        consts_in = m.sem("consts_in")
        o_in = m.sems("o_in", S)
        steps = m.sem("steps")
        normed = m.sem("normed")
        turned = m.sem("turned")
        copied = m.sem("copied")
        stored = m.sems("stored", S)
        block = m.block()
        n_i = TOK // P // S
        STEPS = 3 + RSQRT_STEPS

        @block.sync
        def _(sp):
            sp.dma_start(gain[:, :], gains_dram).then_inc(consts_in, 16)
            sp.dma_start(ident[:, :], ident_dram).then_inc(consts_in, 16)
            for g, (t0, t1) in enumerate(((0, SEQS[0]), (SEQS[0], TOK))):
                heads = diff_o[g][2 * CH:, :].rearrange("(h t) v -> t h v", h=H)
                with sp.Fori(0, (t1 - t0) // P // S) as i:
                    for b in range(S):
                        sp.wait_ge(turned, i * S + t0 // P)
                        sp.dma_start(o[:, b, 0], heads[bass.ds(i * (S * P) + b * P, P)]).then_inc(o_in[b], 16)
                        sp.dma_start(o[:, b, 1].rearrange("p h v -> p (h v)"), cross_o[bass.ds(i * (S * P) + (b * P + t0), P), :]).then_inc(o_in[b], 16)

        @block.vector
        def _(dve):
            dve.wait_ge(consts_in, 32)
            dve.tensor_scalar(gain[:, :], gain[:, :], 1.0 - LAMBDA_INIT, None, ALU.mult).then_inc(steps, 1)
            with dve.Fori(0, n_i) as i:
                for b in range(S):
                    dve.wait_ge(o_in[b], i * (16 * NO) + 16 * NO)
                    dve.wait_ge(normed, i * S + b)
                    step = Chain(dve, steps, (i * S + b) * STEPS + 1)
                    step(dve.tensor_tensor(sq[:, :, :], o[:, b, 0], o[:, b, 0], ALU.mult))
                    step(dve.tensor_reduce(stat[:, 0], sq[:, :, :], AXX, ALU.add))
                    step(dve.tensor_scalar(stat[:, 1], stat[:, 0], 1.0 / P, EPS, ALU.mult, ALU.add))
                    rsqrt(step, dve, stat[:, 2], stat[:, 1], stat[:, 3])
                    for h in range(H):
                        done = dve.scalar_tensor_tensor(o[:, b, 0, h], o[:, b, 0, h], stat[:, 2, h:h + 1], gain[:, :], ALU.mult, ALU.mult)
                    done.then_inc(normed, 1)

        @block.tensor
        def _(pe):
            pe.wait_ge(consts_in, 32)
            with pe.Fori(0, n_i) as i:
                for b in range(S):
                    pe.wait_ge(normed, i * S + (b + 1))
                    pe.wait_ge(copied, i * S)
                    for k in range(NO):
                        for h in range(H):
                            done = pe.transpose(t_ps[:, b, k, h * P:(h + 1) * P], o[:, b, k, h], ident[:, :])
                    done.then_inc(turned, 1)

        @block.scalar
        def _(act):
            act.preload_act_table(ACT.Exp)
            with act.Fori(0, n_i) as i:
                for b in range(S):
                    act.wait_ge(turned, i * S + (b + 1))
                    act.wait_ge(stored[b], i * (16 * NO))
                    for k in range(NO):
                        done = act.activation(out[:, b, k], t_ps[:, b, k], ACT.Copy)
                    done.then_inc(copied, 1)
                    act.wait_ge(copied, i * S + (b + 1))
                    for k in range(NO):
                        dst = oT[(k + 1) * H:(k + 2) * H, :, bass.ds(i * (S * P) + b * P, P)].rearrange("h p t -> p h t")
                        act.dma_start(dst, out[:, b, k].rearrange("p (h t) -> p h t", h=H)).then_inc(stored[b], 16)
            for b in range(S):
                act.wait_ge(stored[b], n_i * 16 * NO)


def phase_merge(nc, x_all, hT_hi, hT_lo, oT, w_z, w_gb, w_o, final_gain, ident_dram, y):
    with ExitStack() as ctx:
        m = Mem(nc, ctx, "merge")
        S, NZ, NG, NO, NB, WT = 2, 12, 24, KT, 3, W // P
        UNITS, COMB, TT, NC = NZ + NG + NO, NZ + NG, CH // P, TOK // CH
        RAW = KT + WT
        h_hi, h_lo = (m.sb(f"h_{s}", [P, KT, CH], FP32R) for s in ("hi", "lo"))
        raw = m.sb("raw", [P, S, RAW, P])
        w_hi, w_lo = (m.sb(f"w_{s}", [P, S, RAW, P], FP32R) for s in ("hi", "lo"))
        o = m.sb("o", [P, S, CH])
        br_hi, br_lo = (m.sb(f"br_{s}", [P, NZ, CH], FP32R) for s in ("hi", "lo"))
        me_hi, me_lo = (m.sb(f"me_{s}", [P, KT, CH], FP32R) for s in ("hi", "lo"))
        sig = m.sb("sig", [P, S, CH])
        tmp = m.sb("tmp", [P, CH])
        total = m.sb("total", [P, CH])
        outT = m.sb("outT", [P, NO, CH])
        x = m.sb("x", [P, TT, D])
        sq = m.sb("sq", [P, D])
        gain = m.sb("gain", [P, D])
        ident = m.sb("ident", [P, P])
        stat = m.sb("stat", [P, 4, TT])
        acc = m.ps("acc", [P, S, CH])
        branch_acc = m.ps("branch_acc", [P, S, CH])
        tp = m.ps("tp", [P, S, D])
        consts_in = m.sem("consts_in")
        h_in = m.sems("h_in", KT)
        raw_in = m.sems("raw_in", S)
        o_in = m.sems("o_in", S)
        x_in = m.sems("x_in", TT)
        y_out = m.sems("y_out", TT)
        hi_split = m.sem("hi_split")
        lo_split = m.sem("lo_split")
        unit_done = m.sem("unit_done")
        sig_ready = m.sem("sig_ready")
        combined = m.sem("combined")
        steps = m.sem("steps")
        out_copied = m.sem("out_copied")
        turned = m.sem("turned")
        added = m.sem("added")
        squared = m.sem("squared")
        normed = m.sem("normed")
        block = m.block()
        RAW_PER = UNITS // S
        Z_STEPS, G_STEPS, T_STEPS = 3, 4, RSQRT_STEPS + 1
        STEPS = NZ * Z_STEPS + NO * G_STEPS + T_STEPS

        def load_h(sp, c, k):
            sp.dma_start(h_hi[:, k].bitcast(FP32), hT_hi[k][:, bass.ds(c * CH, CH)]).then_inc(h_in[k], 16)
            sp.dma_start(h_lo[:, k].bitcast(FP32), hT_lo[k][:, bass.ds(c * CH, CH)]).then_inc(h_in[k], 16)

        def load_w(sp, c, n, s, w, i, free):
            if free:
                sp.wait_ge(lo_split, c * UNITS + n + (1 - S))
            sp.dma_start(raw[:, s, 0:w.shape[2]], block3(w, i)).then_inc(raw_in[s], 16)

        def load_o(sp, c, i, s, wait):
            sp.wait_ge(combined, wait)
            sp.dma_start(o[:, s], oT[bass.ds(i, 1), :, bass.ds(c * CH, CH)].rearrange("o p t -> p (o t)")).then_inc(o_in[s], 16)

        @block.sync
        def _(sp):
            sp.dma_start(ident[:, :], ident_dram).then_inc(consts_in, 16)
            sp.dma_start(gain[:, :], final_gain).then_inc(consts_in, 16)
            for k in range(KT):
                load_h(sp, 0, k)

            def store_y(c):
                for t in range(TT):
                    sp.wait_ge(normed, c * TT + (t + 1))
                    sp.dma_start(rows(y, c * CH + t * P, P), x[:, t]).then_inc(y_out[t], 16)

            def chunk(c, first):
                for s in range(S):
                    load_w(sp, c, s, s, w_z, s, not first)
                    load_o(sp, c, s, s, c * COMB)
                with sp.Fori(1, NZ // S) as i:
                    for s in range(S):
                        load_w(sp, c, i * S + s, s, w_z, i * S + s, True)
                        load_o(sp, c, i * S + s, s, c * COMB + i * S + (s + 1 - S))
                if not first:
                    store_y(c - 1)
                with sp.Fori(0, NG // S) as i:
                    for s in range(S):
                        load_w(sp, c, i * S + (NZ + s), s, w_gb, i * S + s, True)
                for i in range(NO):
                    load_w(sp, c, COMB + i, i % S, w_o, i, True)
                    if i < TT:
                        if not first:
                            sp.wait_ge(y_out[i], c * 16)
                        sp.dma_start(x[:, i], rows(x_all, c * CH + i * P, P)).then_inc(x_in[i], 16)
                    sp.wait_ge(unit_done, c * UNITS + COMB)
                    load_h(sp, c + 1, i)

            chunk(0, True)
            with sp.Fori(1, NC) as c:
                chunk(c, False)
            store_y(NC - 1)
            for t in range(TT):
                sp.wait_ge(y_out[t], NC * 16)
            for k in range(KT):
                sp.wait_ge(h_in[k], (NC + 1) * 32)

        def split_hi(act, c, n, s, kt, free=True):
            act.wait_ge(raw_in[s], c * (16 * RAW_PER) + n * (16 // S) + (16 - s * (16 // S)))
            if free:
                act.wait_ge(unit_done, c * UNITS + n + (1 - S))
            act.activation(w_hi[:, s, 0:kt], raw[:, s, 0:kt], ACT.Copy).then_inc(hi_split, 1)

        @block.scalar
        def _(act):
            act.preload_act_table(ACT.Sigmoid)
            split_hi(act, 0, 0, 0, KT, False)

            def gate(c, n, s):
                act.wait_ge(unit_done, c * UNITS + n + 1)
                act.wait_ge(combined, c * COMB + n + (1 - S) if not isinstance(n, int) or n >= S else c * COMB)
                act.activation(sig[:, s], acc[:, s], ACT.Sigmoid).then_inc(sig_ready, 1)

            def copy_out(c, n, s):
                act.wait_ge(unit_done, c * UNITS + n + (COMB + 1))
                act.activation(outT[:, n], acc[:, s], ACT.Copy).then_inc(out_copied, 1)

            def chunk(c, last):
                for n in range(S):
                    split_hi(act, c, n + 1, (n + 1) % S, KT, True)
                    gate(c, n, n)
                with act.Fori(1, NZ // S - 1) as i:
                    for s in range(S):
                        split_hi(act, c, i * S + (s + 1), (s + 1) % S, KT)
                        gate(c, i * S + s, s)
                for n in range(NZ - S, NZ):
                    split_hi(act, c, n + 1, (n + 1) % S, KT if n + 1 < NZ else RAW)
                    gate(c, n, n % S)
                with act.Fori(0, NG // S - 1) as i:
                    for s in range(S):
                        if s == 0:
                            split_hi(act, c, i * S + (NZ + 1), 1, RAW)
                        else:
                            split_hi(act, c, i * S + (NZ + S), 0, RAW)
                        gate(c, i * S + (NZ + s), s)
                for n in range(COMB - S, COMB):
                    split_hi(act, c, n + 1, (n + 1) % S, RAW if n + 1 < COMB else KT)
                    gate(c, n, n % S)
                for n in range(NO):
                    if n + 1 < NO:
                        split_hi(act, c, COMB + n + 1, (n + 1) % S, KT)
                    elif not last:
                        split_hi(act, c + 1, 0, 0, KT)
                    copy_out(c, n, n % S)
                for t in range(TT):
                    act.wait_ge(added, c * TT + (t + 1))
                    act.wait_ge(squared, c * TT + t)
                    act.activation(sq[:, :], x[:, t], ACT.Square, accum_out=stat[:, 0, t:t + 1]).then_inc(squared, 1)

            with act.Fori(0, NC - 1) as c:
                chunk(c, False)
            chunk(NC - 1, True)

        @block.gpsimd
        def _(pool):
            def low(c, n, s, kt):
                pool.wait_ge(hi_split, c * UNITS + n + 1)
                pool.tensor_tensor(w_lo[:, s, 0:kt], raw[:, s, 0:kt], w_hi[:, s, 0:kt], ALU.subtract).then_inc(lo_split, 1)

            with pool.Fori(0, NC) as c:
                for first, count, kt in ((0, NZ, KT), (NZ, NG, RAW), (COMB, NO, KT)):
                    with pool.Fori(0, count // S) as i:
                        for s in range(S):
                            low(c, i * S + (first + s), s, kt)

        @block.tensor
        def _(pe):
            def z_unit(c, n, s, first):
                if first:
                    pe.wait_ge(out_copied, c * NO)
                else:
                    pe.wait_ge(combined, c * COMB + n + (1 - S))
                pe.wait_ge(lo_split, c * UNITS + n + 1)
                for k in range(KT):
                    if first and n == 0:
                        pe.wait_ge(h_in[k], c * 32 + 32)
                    done = product3(pe, acc[:, s], w_hi[:, s, k], w_lo[:, s, k], h_hi[:, k], h_lo[:, k], k == 0, k == KT - 1)
                done.then_inc(unit_done, 1)

            def gb_unit(c, n, s, b):
                pe.wait_ge(combined, c * COMB + n + (1 - S))
                pe.wait_ge(lo_split, c * UNITS + n + 1)
                for k in range(KT):
                    product3(pe, acc[:, s], w_hi[:, s, k], w_lo[:, s, k], h_hi[:, k], h_lo[:, k], k == 0, k == KT - 1)
                for k in range(WT):
                    done = product3(pe, branch_acc[:, s], w_hi[:, s, KT + k], w_lo[:, s, KT + k],
                                    br_hi[:, WT * b + k], br_lo[:, WT * b + k], k == 0, k == WT - 1)
                done.then_inc(unit_done, 1)

            pe.wait_ge(consts_in, 32)
            with pe.Fori(0, NC) as c:
                for n in range(S):
                    z_unit(c, n, n, True)
                with pe.Fori(1, NZ // S) as i:
                    for s in range(S):
                        z_unit(c, i * S + s, s, False)
                with pe.Fori(0, NG // (S * NB)) as i:
                    for j in range(S * NB):
                        gb_unit(c, i * (S * NB) + (NZ + j), j % S, j % NB)
                for n in range(NO):
                    s = n % S
                    if n < S:
                        pe.wait_ge(combined, c * COMB + (COMB + n + 1 - S))
                    else:
                        pe.wait_ge(out_copied, c * NO + (n + 1 - S))
                    pe.wait_ge(lo_split, c * UNITS + (COMB + n + 1))
                    for k in range(KT):
                        if n == 0 and k == KT - 1:
                            pe.wait_ge(combined, c * COMB + COMB)
                        done = product3(pe, acc[:, s], w_hi[:, s, k], w_lo[:, s, k], me_hi[:, k], me_lo[:, k], k == 0, k == KT - 1)
                    done.then_inc(unit_done, 1)
                pe.wait_ge(out_copied, c * NO + NO)
                for t in range(TT):
                    pe.wait_ge(added, c * TT + max(t + 1 - S, 0))
                    for k in range(NO):
                        done = pe.transpose(tp[:, t % S, k * P:(k + 1) * P], outT[:, k, t * P:(t + 1) * P], ident[:, :])
                    done.then_inc(turned, 1)

        @block.vector
        def _(dve):
            dve.wait_ge(consts_in, 32)
            with dve.Fori(0, NC) as c:
                with dve.Fori(0, NZ // S) as i:
                    for s in range(S):
                        step = Chain(dve, steps, c * STEPS + i * (S * Z_STEPS) + s * Z_STEPS)
                        n = i * S + s
                        dve.wait_ge(sig_ready, c * COMB + i * S + (s + 1))
                        dve.wait_ge(o_in[s], c * (16 * NZ // S) + i * 16 + 16)
                        step(dve.tensor_tensor(tmp[:, :], acc[:, s], sig[:, s], ALU.mult))
                        step(dve.tensor_tensor(total[:, :], tmp[:, :], o[:, s], ALU.mult))
                        step(dve.tensor_copy(br_hi[:, bass.ds(n, 1)].rearrange("p a t -> p (a t)"), total[:, :]))
                        dve.tensor_tensor(br_lo[:, bass.ds(n, 1)].rearrange("p a t -> p (a t)"), total[:, :],
                                          br_hi[:, bass.ds(n, 1)].rearrange("p a t -> p (a t)"), ALU.subtract).then_inc(combined, 1)
                with dve.Fori(0, NG // (S * NB)) as i:
                    for j in range(S * NB):
                        s, b, d = j % S, j % NB, j // NB
                        n = i * (S * NB) + (NZ + j)
                        if b == 0:
                            step = Chain(dve, steps, c * STEPS + i * (S * G_STEPS) + (NZ * Z_STEPS + d * G_STEPS))
                        dve.wait_ge(sig_ready, c * COMB + n + 1)
                        dve.wait_ge(combined, c * COMB + n)
                        if b == 0:
                            dve.tensor_tensor(total[:, :], branch_acc[:, s], sig[:, s], ALU.mult).then_inc(combined, 1)
                            continue
                        step(dve.tensor_tensor(tmp[:, :], branch_acc[:, s], sig[:, s], ALU.mult))
                        if b == 1:
                            dve.tensor_tensor(total[:, :], total[:, :], tmp[:, :], ALU.add).then_inc(combined, 1)
                            continue
                        step(dve.tensor_tensor(total[:, :], total[:, :], tmp[:, :], ALU.add))
                        hi = me_hi[:, bass.ds(i * S + d, 1)].rearrange("p a t -> p (a t)")
                        lo = me_lo[:, bass.ds(i * S + d, 1)].rearrange("p a t -> p (a t)")
                        step(dve.tensor_copy(hi, total[:, :]))
                        dve.tensor_tensor(lo, total[:, :], hi, ALU.subtract).then_inc(combined, 1)
                for t in range(TT):
                    dve.wait_ge(turned, c * TT + (t + 1))
                    dve.wait_ge(x_in[t], c * 16 + 16)
                    dve.tensor_tensor(x[:, t], tp[:, t % S], x[:, t], ALU.add).then_inc(added, 1)
                step = Chain(dve, steps, c * STEPS + (NZ * Z_STEPS + NO * G_STEPS))
                dve.wait_ge(squared, c * TT + TT)
                step(dve.tensor_scalar(stat[:, 1], stat[:, 0], 1.0 / D, EPS, ALU.mult, ALU.add))
                rsqrt(step, dve, stat[:, 2], stat[:, 1], stat[:, 3])
                for t in range(TT):
                    dve.scalar_tensor_tensor(x[:, t], x[:, t], stat[:, 2, t:t + 1], gain[:, :], ALU.mult, ALU.mult).then_inc(normed, 1)


def build(nc, x_all, gains, w_stream, w_glr, w_values, w_mem, w_mem_values, w2, gla_sums, gla_picked, gla_diag,
          gla_gain, alibi, slopes, lambdas, diff_gain, w_z, w_gb, w_o, final_gain, ident, y):
    def scratch(name, *shape):
        return nc.dram_tensor(f"scratch_{name}", shape, FP32, kind="Internal").ap()

    hT_hi, hT_lo = scratch("hT_hi", KT, P, ROWS), scratch("hT_lo", KT, P, ROWS)
    featT, glrT = scratch("featT", N_FEAT, P, TOK), scratch("glrT", P, TOK)
    memkT, mem_v = scratch("memkT", H, P, MEM), scratch("mem_v", MEM, W)
    gla_v, diff_v = scratch("gla_v", TOK, W), scratch("diff_v", TOK, W)
    L_hi, L_lo = scratch("L_hi", TOK, W), scratch("L_lo", TOK, W)
    gla_o, cross_o = scratch("gla_o", TOK, W), scratch("cross_o", TOK, W)
    diff_o = [scratch(f"diff_o{g}", 2 * CH + H * T, P) for g, T in enumerate(SEQS)]
    qb, kb, decb = scratch("qb", TOK, H * GK), scratch("kb", TOK, H * GK), scratch("decb", TOK, H // 2)
    oT = scratch("oT", 3 * H, P, TOK)

    phase_norm(nc, x_all, gains, ident, hT_hi, hT_lo)
    phase_project(nc, "proj", hT_hi, hT_lo, 0, TOK // CH, w_stream, N_FEAT, [w_glr], [w_values[0], w_values[1]],
                  featT, [glrT], [gla_v, diff_v])
    phase_project(nc, "mem", hT_hi, hT_lo, TOK, 1, w_mem, H, [], [w_mem_values], memkT, [], [mem_v])
    phase_decay(nc, glrT, w2, L_hi, L_lo)
    phase_gla_forward(nc, featT, L_hi, L_lo, gla_v, gla_sums, gla_picked, gla_diag, ident, gla_o, qb, kb, decb)
    phase_gla_backward(nc, gla_v, gla_o, qb, kb, decb, gla_gain, ident, oT)
    for g, T in enumerate(SEQS):
        phase_diff(nc, f"diff{g}", featT, diff_v, sum(SEQS[:g]), T, alibi, slopes, lambdas, ident, diff_o[g])
    phase_cross(nc, featT, memkT, mem_v, ident, cross_o)
    phase_heads(nc, diff_o, cross_o, diff_gain, ident, oT)
    phase_merge(nc, x_all, hT_hi, hT_lo, oT, w_z, w_gb, w_o, final_gain, ident, y)


OFFSETS = dict(zip(
    ("g_q", "g_k", "g_v", "g_lr", "z_a", "d_q", "d_k", "d_v", "z_b", "c_q", "z_c", "gate"),
    np.cumsum([0, H * GK, H * GK, W, 2 * RANK, W, W, W, W, W, W, W]).tolist()))


def column_block(w, start, width=P):
    return np.ascontiguousarray(w[:, start:start + width].reshape(-1, P, width).transpose(1, 0, 2))


def blocks(w, start, n):
    return [column_block(w, start + P * j) for j in range(n)]


def on_partitions(a):
    return np.ascontiguousarray(np.broadcast_to(a, (P, *a.shape)))


def layout(x_prompt, x_sample, mem_prompt, mem_sample, norm_g, w_in, gla_gate_w2, gla_gate_b, gla_norm_g,
           diff_lambda, diff_norm_g, mem_norm_g, w_mem_kv, w_branch, w_out, final_norm_g):
    w, at = w_in[0], OFFSETS
    w2 = np.zeros((2 * RANK + 1, 2, H * GK), w.dtype)
    for d in range(2):
        w2[d * RANK:(d + 1) * RANK, d] = gla_gate_w2[0, d]
        w2[2 * RANK, d] = gla_gate_b[0, d]
    sums, picked = gla_matrices()
    distance = np.abs(np.arange(ALIBI_W)[None, :] - ALIBI_MID - np.arange(P)[:, None])
    slopes = np.array([[64 ** -0.5 / s, s, -s] for s in (1.0, *SLOPES, 1.0)], np.float32)
    return {
        "x_all": np.concatenate([x_prompt[0], x_sample[0], mem_prompt[0], mem_sample[0]]),
        "gains": on_partitions(np.stack([norm_g[0], mem_norm_g[0]])),
        "w_stream": np.stack(blocks(w, at["g_q"], 2) + blocks(w, at["g_k"], 2) + blocks(w, at["d_q"], H)
                             + blocks(w, at["d_k"], H) + blocks(w, at["c_q"], H)),
        "w_glr": column_block(w, at["g_lr"]),
        "w_values": np.stack([column_block(w, at["g_v"], W), column_block(w, at["d_v"], W)]),
        "w_mem": np.stack(blocks(w_mem_kv[0], 0, H)),
        "w_mem_values": column_block(w_mem_kv[0], W, W),
        "w2": w2.reshape(2 * RANK + 1, -1),
        "gla_sums": sums.reshape(P, 2, -1),
        "gla_picked": picked,
        "gla_diag": 2 * np.eye(P, dtype=np.float32),
        "gla_gain": on_partitions(gla_norm_g[0]),
        "alibi": (-distance).astype(np.float32),
        "slopes": on_partitions(slopes),
        "lambdas": on_partitions(diff_lambda[0].reshape(2, 2, -1)),
        "diff_gain": on_partitions(diff_norm_g[0]),
        "w_z": np.stack(blocks(w, at["z_a"], H) + blocks(w, at["z_b"], H) + blocks(w, at["z_c"], H)),
        "w_gb": np.stack([np.concatenate([column_block(w, at["gate"] + b * D + d * P), column_block(w_branch[0, b], d * P)], 1)
                          for d in range(KT) for b in range(3)]),
        "w_o": np.stack(blocks(w_out[0], 0, KT)),
        "final_gain": on_partitions(final_norm_g),
        "ident": np.eye(P, dtype=np.float32),
    }


def kernel(**inputs):
    import concourse.bacc as bacc
    from concourse.bass_utils import run_bass_kernel_spmd

    nc = bacc.Bacc("TRN2", target_bir_lowering=False, num_devices=1)
    arrays = {k: np.ascontiguousarray(a) for k, a in layout(**{k: np.asarray(a) for k, a in inputs.items()}).items()}
    args = {k: nc.dram_tensor(f"in_{k}", a.shape, mybir.dt.from_np(a.dtype), kind="ExternalInput").ap() for k, a in arrays.items()}
    y = nc.dram_tensor("out_y", (TOK, D), FP32, kind="ExternalOutput").ap()
    build(nc, y=y, **args)
    r = run_bass_kernel_spmd(nc, [{f"in_{k}": a for k, a in arrays.items()}], core_ids=[0])
    got = np.asarray(r.results[0]["out_y"])
    return got[None, :SEQS[0]], got[None, SEQS[0]:]
```
